# Optimizing a Trainium2 kernel written in Bass

```python
import math
import jax, jax.numpy as jnp
from jax import lax
import numpy as np

D_MODEL = 1024
BATCH = 1
SEQ = 256
DEPTH = 1

POOL_WINDOWS = (2, 4, 8, 16)
POOL_GROUPS = len(POOL_WINDOWS)
POOL_GROUP_W = 128
POOL_W = POOL_GROUPS * POOL_GROUP_W
GDN_HEADS = 8
GDN_DK = 128
GDN_DV = 128
GDN_W = GDN_HEADS * GDN_DK
GDN_CONV = 4
GDN_CHUNK = 64
N_BRANCH = 2
IN_SPLITS = (POOL_W,
             POOL_W + 3 * GDN_W,
             POOL_W + 4 * GDN_W,
             POOL_W + 4 * GDN_W + GDN_HEADS,
             POOL_W + 4 * GDN_W + 2 * GDN_HEADS)
IN_W = POOL_W + 4 * GDN_W + 2 * GDN_HEADS + N_BRANCH * D_MODEL
N_EXPERTS = 32
TOP_K = 4
EXPERT_HIDDEN = D_MODEL
SWIGLU_LIMIT = 7.0
SWIGLU_ALPHA = 1.702
MOE_BLOCK = 128
RMS_EPS = 1e-6
ADA_INIT_SCALE = 0.5

kernel_name = "hybrid_pool_gdn_moe_adaln"

def rmsnorm(x, g):
    xf = x.astype(jnp.float32)
    y = xf * lax.rsqrt(jnp.mean(xf * xf, axis=-1, keepdims=True) + RMS_EPS)
    return (y * g.astype(jnp.float32)).astype(x.dtype)

def l2norm(x):
    xf = x.astype(jnp.float32)
    return xf * lax.rsqrt(jnp.sum(xf * xf, axis=-1, keepdims=True) + RMS_EPS)

def multiscale_pool(u, pool_w, pool_scale):
    b, s, _ = u.shape
    uf = u.astype(jnp.float32)
    cs = jnp.cumsum(uf, axis=1)
    count = jnp.arange(1, s + 1, dtype=jnp.float32)[None, :, None]
    outs = []
    for gi, w in enumerate(POOL_WINDOWS):
        sl = slice(gi * POOL_GROUP_W, (gi + 1) * POOL_GROUP_W)
        cg = cs[..., sl]
        lag = jnp.pad(cg, ((0, 0), (w, 0), (0, 0)))[:, :s]
        mean = (cg - lag) / jnp.minimum(count, float(w))
        outs.append(mean - uf[..., sl])
    pooled = jnp.stack(outs, axis=2)
    y = jnp.einsum('bsgc,gcd->bsgd', pooled, pool_w.astype(jnp.float32)).reshape(b, s, POOL_W)
    return (y * pool_scale.astype(jnp.float32)).astype(u.dtype)

def gated_delta_rule_chunked(q, k, v, g, beta):
    b, h, s, dk = q.shape
    dv = v.shape[-1]
    nc = s // GDN_CHUNK
    q = q * (dk ** -0.5)
    q, k, v = (t.reshape(b, h, nc, GDN_CHUNK, t.shape[-1]) for t in (q, k, v))
    beta = beta.reshape(b, h, nc, GDN_CHUNK)
    g = jnp.cumsum(g.reshape(b, h, nc, GDN_CHUNK), axis=-1)
    idx = jnp.arange(GDN_CHUNK)
    causal = idx[:, None] >= idx[None, :]
    strict = idx[:, None] > idx[None, :]
    gdiff = g[..., :, None] - g[..., None, :]
    decay = jnp.where(causal, jnp.exp(jnp.where(causal, gdiff, 0.0)), 0.0)
    k_beta = k * beta[..., None]
    kk = jnp.einsum('bhnik,bhnjk->bhnij', k_beta, k) * decay
    lhs = jnp.where(strict, kk, 0.0) + jnp.eye(GDN_CHUNK, dtype=kk.dtype)
    rhs = jnp.concatenate([v * beta[..., None], k_beta * jnp.exp(g)[..., None]], axis=-1)
    sol = lax.linalg.triangular_solve(lhs, rhs, left_side=True, lower=True)
    u, w = sol[..., :dv], sol[..., dv:]
    attn_intra = jnp.einsum('bhnik,bhnjk->bhnij', q, k) * decay
    q_dec = q * jnp.exp(g)[..., None]
    g_last = g[..., -1]
    k_dec = k * jnp.exp(g_last[..., None] - g)[..., None]

    def step(state, inp):
        q_i, k_i, u_i, w_i, a_i, gl_i = inp
        v_new = u_i - jnp.einsum('bhck,bhkv->bhcv', w_i, state)
        o = jnp.einsum('bhck,bhkv->bhcv', q_i, state) + jnp.einsum('bhij,bhjv->bhiv', a_i, v_new)
        state = state * jnp.exp(gl_i)[..., None, None] + jnp.einsum('bhck,bhcv->bhkv', k_i, v_new)
        return state, o

    mv = lambda t: jnp.moveaxis(t, 2, 0)
    s0 = jnp.zeros((b, h, dk, dv), jnp.float32)
    _, o = lax.scan(step, s0, (mv(q_dec), mv(k_dec), mv(u), mv(w), mv(attn_intra), mv(g_last)))
    return jnp.moveaxis(o, 0, 2).reshape(b, h, s, dv)

def hybrid_mixer(h, w_in, conv_w, pool_w, pool_scale, a_log, dt_bias, gdn_norm_g,
                 w_pool_out, w_gdn_out, w_out):
    b, s, _ = h.shape
    proj = h @ w_in
    u_pool, qkv, z, beta_in, a_in, gate_in = jnp.split(proj, IN_SPLITS, axis=-1)

    y_pool = multiscale_pool(u_pool, pool_w, pool_scale)

    qkv = lax.conv_general_dilated(qkv, conv_w[:, None, :].astype(qkv.dtype), window_strides=(1,),
                                   padding=[(GDN_CONV - 1, 0)],
                                   dimension_numbers=('NWC', 'WIO', 'NWC'),
                                   feature_group_count=qkv.shape[-1])
    qkv = jax.nn.silu(qkv)
    q, k, v = jnp.split(qkv, 3, axis=-1)
    heads = lambda t: jnp.transpose(t.reshape(b, s, GDN_HEADS, -1), (0, 2, 1, 3))
    q = heads(l2norm(q.reshape(b, s, GDN_HEADS, GDN_DK)).reshape(b, s, GDN_W))
    k = heads(l2norm(k.reshape(b, s, GDN_HEADS, GDN_DK)).reshape(b, s, GDN_W))
    v = heads(v.astype(jnp.float32))
    beta = jnp.transpose(jax.nn.sigmoid(beta_in.astype(jnp.float32)), (0, 2, 1))
    g = -jnp.exp(a_log.astype(jnp.float32)) * jax.nn.softplus(a_in.astype(jnp.float32) + dt_bias.astype(jnp.float32))
    g = jnp.transpose(g, (0, 2, 1))
    o = gated_delta_rule_chunked(q, k, v, g, beta)
    o = jnp.transpose(o, (0, 2, 1, 3))
    o = rmsnorm(o, gdn_norm_g) * jax.nn.silu(z.astype(jnp.float32)).reshape(b, s, GDN_HEADS, GDN_DV)
    y_gdn = o.reshape(b, s, GDN_W).astype(h.dtype)

    gates = jax.nn.sigmoid(gate_in.astype(jnp.float32)).reshape(b, s, N_BRANCH, D_MODEL).astype(h.dtype)
    y = gates[:, :, 0] * (y_pool @ w_pool_out) + gates[:, :, 1] * (y_gdn @ w_gdn_out)
    return y @ w_out

def moe_ffn(h, router_w, router_b, w1, b1, w2, b2):
    b, s, d = h.shape
    t = b * s
    tk = t * TOP_K
    xt = h.reshape(t, d)
    logits = (xt @ router_w + router_b).astype(jnp.float32)
    top_val, top_idx = lax.top_k(logits, TOP_K)
    comb = jax.nn.softmax(top_val, axis=-1)
    flat_e = top_idx.reshape(tk)
    order = jnp.argsort(flat_e)
    e_sorted = flat_e[order]
    tok_sorted = (order // TOP_K).astype(jnp.int32)
    w_sorted = comb.reshape(tk)[order]
    sizes = jnp.bincount(flat_e, length=N_EXPERTS)
    padded = ((sizes + MOE_BLOCK - 1) // MOE_BLOCK) * MOE_BLOCK
    start = jnp.cumsum(sizes) - sizes
    pend = jnp.cumsum(padded)
    pstart = pend - padded
    dest = pstart[e_sorted] + (jnp.arange(tk) - start[e_sorted])
    n_blocks = -(-tk // MOE_BLOCK) + N_EXPERTS
    buf_tok = jnp.full((n_blocks * MOE_BLOCK,), t, jnp.int32).at[dest].set(tok_sorted)
    buf_w = jnp.zeros((n_blocks * MOE_BLOCK,), jnp.float32).at[dest].set(w_sorted)
    blk_e = jnp.minimum(jnp.searchsorted(pend, jnp.arange(n_blocks) * MOE_BLOCK, side='right'),
                        N_EXPERTS - 1)
    xpad = jnp.concatenate([xt, jnp.zeros((1, d), xt.dtype)], axis=0)

    def expert_block(args):
        tok_b, e = args
        xb = xpad[tok_b]
        hu = xb @ w1[e] + b1[e]
        x_glu = jnp.minimum(hu[:, 0::2], SWIGLU_LIMIT)
        x_lin = jnp.clip(hu[:, 1::2], -SWIGLU_LIMIT, SWIGLU_LIMIT)
        act = x_glu * jax.nn.sigmoid(SWIGLU_ALPHA * x_glu) * (x_lin + 1.0)
        return act @ w2[e] + b2[e]

    ys = lax.map(expert_block, (buf_tok.reshape(n_blocks, MOE_BLOCK), blk_e))
    ys = ys.reshape(n_blocks * MOE_BLOCK, d) * buf_w[:, None].astype(ys.dtype)
    out = jax.ops.segment_sum(ys, buf_tok, num_segments=t + 1)[:t]
    return out.reshape(b, s, d)

def setup_inputs(seed: int = 0) -> dict:
    key = jax.random.key(seed)
    ks = jax.random.split(key, 26)
    L, D = DEPTH, D_MODEL
    nrm = lambda k, shape: jax.random.normal(k, shape, jnp.float32)
    fan = lambda k, shape, fan_in: nrm(k, shape) * fan_in ** -0.5
    dt = jnp.exp(jax.random.uniform(ks[11], (L, GDN_HEADS), jnp.float32,
                                    minval=math.log(1e-3), maxval=math.log(1e-1)))
    return {
        "x": nrm(ks[0], (BATCH, SEQ, D)),
        "c": nrm(ks[1], (BATCH, D)),
        "ada_w": fan(ks[2], (L, D, 6 * D), D) * ADA_INIT_SCALE,
        "ada_b": 0.01 * nrm(ks[3], (L, 6 * D)),
        "norm_mix_g": 1.0 + 0.05 * nrm(ks[4], (L, D)),
        "norm_ffn_g": 1.0 + 0.05 * nrm(ks[5], (L, D)),
        "w_in": fan(ks[6], (L, D, IN_W), D),
        "conv_w": fan(ks[7], (L, GDN_CONV, 3 * GDN_W), GDN_CONV),
        "pool_w": fan(ks[8], (L, POOL_GROUPS, POOL_GROUP_W, POOL_GROUP_W), POOL_GROUP_W),
        "pool_scale": 1.0 + 0.05 * nrm(ks[9], (L, POOL_W)),
        "a_log": jnp.log(jax.random.uniform(ks[10], (L, GDN_HEADS), jnp.float32, minval=1.0, maxval=16.0)),
        "dt_bias": dt + jnp.log(-jnp.expm1(-dt)),
        "gdn_norm_g": 1.0 + 0.05 * nrm(ks[12], (L, GDN_DV)),
        "w_pool_out": fan(ks[13], (L, POOL_W, D), POOL_W),
        "w_gdn_out": fan(ks[14], (L, GDN_W, D), GDN_W),
        "w_out": fan(ks[15], (L, D, D), D),
        "router_w": fan(ks[16], (L, D, N_EXPERTS), D),
        "router_b": 0.01 * nrm(ks[17], (L, N_EXPERTS)),
        "exp_w1": fan(ks[18], (L, N_EXPERTS, D, 2 * EXPERT_HIDDEN), D),
        "exp_b1": 0.01 * nrm(ks[19], (L, N_EXPERTS, 2 * EXPERT_HIDDEN)),
        "exp_w2": fan(ks[20], (L, N_EXPERTS, EXPERT_HIDDEN, D), EXPERT_HIDDEN),
        "exp_b2": 0.01 * nrm(ks[21], (L, N_EXPERTS, D)),
        "final_norm_g": 1.0 + 0.05 * nrm(ks[22], (D,)),
    }

def reference(x, c, ada_w, ada_b, norm_mix_g, norm_ffn_g, w_in, conv_w, pool_w, pool_scale,
              a_log, dt_bias, gdn_norm_g, w_pool_out, w_gdn_out, w_out, router_w, router_b,
              exp_w1, exp_b1, exp_w2, exp_b2, final_norm_g):
    c_act = jax.nn.silu(c)
    for l in range(DEPTH):
        mod = (c_act @ ada_w[l] + ada_b[l])[:, None, :]
        sh1, sc1, gt1, sh2, sc2, gt2 = jnp.split(mod, 6, axis=-1)
        h = rmsnorm(x, norm_mix_g[l]) * (1.0 + sc1) + sh1
        x = x + gt1 * hybrid_mixer(h, w_in[l], conv_w[l], pool_w[l], pool_scale[l], a_log[l], dt_bias[l],
                                   gdn_norm_g[l], w_pool_out[l], w_gdn_out[l], w_out[l])
        h = rmsnorm(x, norm_ffn_g[l]) * (1.0 + sc2) + sh2
        x = x + gt2 * moe_ffn(h, router_w[l], router_b[l], exp_w1[l], exp_b1[l], exp_w2[l], exp_b2[l])
    return rmsnorm(x, final_norm_g)


_drawn_inputs = setup_inputs


def setup_inputs(seed=0):
    import zlib

    import numpy as np

    out = dict(_drawn_inputs(seed))
    spreads = {}
    factors = {'ada_b': 3.364,
     'norm_mix_g': 3.447,
     'pool_scale': 5.152,
     'a_log': 3.572,
     'gdn_norm_g': 7.455,
     'router_b': 49.232,
     'exp_b1': 64.0,
     'exp_b2': 64.0,
     'norm_ffn_g': 8.0}
    for name, (base, spread) in spreads.items():
        noise = np.random.default_rng([zlib.crc32(name.encode()), seed]).standard_normal(out[name].shape)
        drawn = base * np.exp(spread * noise) if base else spread * noise
        out[name] = __import__('jax').numpy.asarray(drawn.astype(out[name].dtype))
    for name, factor in factors.items():
        out[name] = (out[name] * factor).astype(out[name].dtype)
    return out
```

```python
from contextlib import ExitStack

import numpy as np
import concourse.bass as bass
from concourse import mybir

F32 = mybir.dt.float32
I32 = mybir.dt.int32
U32 = mybir.dt.uint32
ALU = mybir.AluOpType
ACT = mybir.ActivationFunctionType
AX = mybir.AxisListType

P = 128
D = 1024
S = 256
T = S // P
KC = D // P
HEADS = 8
HG = 4
CHUNK = 64
WINDOWS = (2, 4, 8, 16)
POOL_W = 512
GDN_W = 1024
TAPS = 4
E = 32
TOPK = 4
SLOTS = 80
ROUNDS = -(-S // SLOTS)
RING = 6
CW = 512
EPS = 1e-6
LIMIT = 7.0
ALPHA = 1.702

COL_POOL = 0
COL_QKV = POOL_W
COL_Z = COL_QKV + 3 * GDN_W
COL_BA = COL_Z + GDN_W
COL_GATE = COL_BA + 2 * HEADS

ROW_ADA_B = 0
ROW_C = 48
ROW_G1 = 56
ROW_G2 = 64
ROW_POOL = 72
ROW_GDN = 76
ROWS = 77

CONST = {}
_at = 0
for _name, _w in (("ident", P), ("ones", P), ("causal", P), ("after", P), ("strict", P), ("before", P),
                  ("off1", P), ("off1T", P), ("off2T", P), ("off4T", P), ("off8T", P), ("off16T", P),
                  ("off32T", P), ("iota", SLOTS), ("count", len(WINDOWS) * 16)):
    CONST[_name] = (_at, _w)
    _at += _w
CONST_W = _at


def constants():
    c = np.zeros((P, CONST_W), np.float32)
    r, q = np.meshgrid(np.arange(P), np.arange(P), indexing="ij")
    same = r // CHUNK == q // CHUNK

    def put(name, a):
        o, w = CONST[name]
        c[:, o:o + w] = a

    put("ident", r == q)
    put("ones", 1.0)
    put("causal", same & (r <= q))
    put("after", same & (r > q))
    put("strict", same & (r > q))
    put("before", r < q)
    for s in (1, 2, 4, 8, 16, 32):
        off = (r // (2 * s) == q // (2 * s)) & (q // s % 2 == 1) & (r // s % 2 == 0)
        put(f"off{s}T", off)
        if s == 1:
            put("off1", off.T)
    put("iota", np.arange(SLOTS))
    t = np.arange(16)
    put("count", np.concatenate([1.0 / np.minimum(t + 1, w) for w in WINDOWS]))
    return c


def program(nc, x, c, ada_w, ada_b, norm_mix_g, norm_ffn_g, w_in, conv_w, pool_w, pool_scale, a_log,
            dt_bias, gdn_norm_g, w_pool_out, w_gdn_out, w_out, router_w, router_b, exp_w1, exp_b1,
            exp_w2, exp_b2, final_norm_g, const, out):
    with ExitStack() as ctx:
        ctx.enter_context(nc.allow_non_contiguous_dma(reason="small parameter rows"))

        def sb(name, shape, dt=F32):
            return ctx.enter_context(nc.sbuf_tensor(name, shape, dt))

        def sem(name):
            return ctx.enter_context(nc.semaphore(name))

        ring = sb("ring", [P, RING, KC, CW])
        consts = sb("consts", [P, CONST_W])
        region_x = sb("region_x", [P, 2048])
        region_h = sb("region_h", [P, 2048])
        qkv = sb("qkv", [P, 24, S])
        region_y = sb("region_y", [P, KC, S])
        region_z = sb("region_z", [P, HEADS, S])
        work = sb("work", [P, 9728])
        cols = sb("cols", [P, ROWS])
        conv_cols = sb("conv_cols", [P, TAPS, 24])
        mod = sb("mod", [P, 48])
        scale1 = sb("scale1", [P, KC])
        scale2 = sb("scale2", [P, KC])
        c_act = sb("c_act", [P, KC])
        b1_cols = sb("b1_cols", [P, E, 4, 4])
        b2_cols = sb("b2_cols", [P, KC, E])
        rw = sb("rw", [P, KC, E])
        rb = sb("rb", [P, E])
        stat = sb("stat", [P, 2, 4])
        heads_in = sb("heads_in", [P, 12, T, HEADS])
        top = sb("top", [P, T, 8])
        top_i = sb("top_i", [P, T, 8], U32)
        small = sb("small", [P, 48])
        rounds_i = sb("rounds_i", [P, 1], I32)

        def const_tile(name):
            o, w = CONST[name]
            return consts[:, o:o + w]

        ident = const_tile("ident")
        ones = const_tile("ones")

        def over_heads(tile):
            return tile.unsqueeze(1).to_broadcast([P, HG, P])

        def per_head(a):
            return a.unsqueeze(2).to_broadcast([P, HG, P])

        xt = region_x[:, :].rearrange("p (t d) -> p t d", t=T)
        hT = region_h[:, :].rearrange("p (c s) -> p c s", c=KC)
        q_of, k_of, v_of = (qkv[:, i * HEADS:(i + 1) * HEADS, :] for i in range(3))
        BETA, APLUS, MAG, EMAG, ONEP, LN1P, G, GC, GL, EG, KDF, BEG = range(12)

        def head_col(what, t, h):
            return heads_in[:, what, t, h:h + 1]

        sq = work[:, 0:4096].rearrange("p (i n) -> p i n", i=8)
        u_pool = work[:, 4096:5120].rearrange("p (g s) -> p g s", g=4)
        pool_a = work[:, 5120:6144].rearrange("p (g s) -> p g s", g=4)
        pool_b = work[:, 6144:7168].rearrange("p (g s) -> p g s", g=4)
        y_pool = work[:, 7168:8192].rearrange("p (g s) -> p g s", g=4)
        pw = work[:, 8192:8704].rearrange("p (g n) -> p g n", g=4)
        wba = work[:, 8704:8832].rearrange("p (c n) -> p c n", c=KC)
        rows = work[:, 8832:8960]
        conv_rows = work[:, 8960:9088]
        b1_rows = work[:, 0:2048]
        b2_rows = work[:, 2048:3072]

        def matrices(tensor, i):
            return tensor[:, i * 1024:(i + 1) * 1024].rearrange("p (t h n) -> p t h n", t=T, h=HG)

        decay = matrices(region_x, 0)
        decayT = matrices(region_x, 1)
        lT, inv, invT, prod, off, eg_row, vb, kbg, kdec = (matrices(work, i) for i in range(9))
        state = work[:, 9216:9728].rearrange("p (h n) -> p h n", h=HG)
        o_nat = qkv[:, 16:24, :].rearrange("p (g a) s -> p g (a s)", g=2) \
            .rearrange("p g (t h n) -> p g t h n", t=T, h=HG)
        o_sq = work[:, 0:2048]

        gate1 = k_of
        moT = q_of
        xn2 = k_of.rearrange("p h s -> p (h s)").rearrange("p (t d) -> p t d", t=T)
        h2T = hT
        h2 = v_of.rearrange("p h s -> p (h s)").rearrange("p (t d) -> p t d", t=T)

        m = 0

        def take(n, parts=P):
            nonlocal m
            a = work[0:parts, m:m + n]
            m += n
            return a

        b8 = region_y[:, :, :].rearrange("p c s -> p (c s)")
        sel = take(T * SLOTS).rearrange("p (t s) -> p t s", t=T)
        wsel = take(T * SLOTS).rearrange("p (t s) -> p t s", t=T)
        wselT = take(T * P, SLOTS)
        xT = take(KC * SLOTS).rearrange("p (c s) -> p c s", c=KC)
        actT = take(KC * SLOTS).rearrange("p (c s) -> p c s", c=KC)
        yT = take(KC * SLOTS).rearrange("p (c s) -> p c s", c=KC)
        y_nat = take(D, SLOTS)
        hu = take(4 * SLOTS).rearrange("p (b s) -> p b s", b=4)
        sig = take(2 * SLOTS).rearrange("p (b s) -> p b s", b=2)
        fin = take(T * D).rearrange("p (t d) -> p t d", t=T)
        fin_g = take(D)
        logits = b8[:, 0:64].rearrange("p (t e) -> p t e", t=T)
        idx = b8[:, 96:112].rearrange("p (t n) -> p t n", t=T)
        hot = b8[:, 128:192].rearrange("p (t e) -> p t e", t=T)
        mask = b8[:, 192:256].rearrange("p (t e) -> p t e", t=T)
        gatew = b8[:, 256:320].rearrange("p (t e) -> p t e", t=T)
        slot_of = b8[:, 320:386].rearrange("p (t e) -> p t e", t=T)
        expw = b8[:, 452:468].rearrange("p (t n) -> p t n", t=T)

        bank = [ctx.enter_context(nc.psum_tensor(f"bank{i}", [P, 512], F32)) for i in range(8)]

        def pair(i):
            return bank[i][:, :].rearrange("p (a s) -> p a s", a=2)

        def quad(i):
            return bank[i][:, :].rearrange("p (h n) -> p h n", h=HG)

        const_in = sem("const_in")
        rows_in = sem("rows_in")
        x_in = sem("x_in")
        early_in = sem("early_in")
        b_in = sem("b_in")
        fin_in = sem("fin_in")
        out_done = sem("out_done")
        landed = [sem(f"landed{i}") for i in range(RING)]
        used = [sem(f"used{i}") for i in range(RING)]

        vec_chain = sem("vec_chain")
        act_chain = sem("act_chain")
        pool_chain = sem("pool_chain")

        pe_rows = sem("pe_rows")
        vec_cols = sem("vec_cols")
        act_c = sem("act_c")
        act_xsq = sem("act_xsq")
        act_xrms = sem("act_xrms")
        vec_xn = sem("vec_xn")
        pe_xT = sem("pe_xT")
        pe_ada = sem("pe_ada")
        vec_mod = sem("vec_mod")
        vec_hT = sem("vec_hT")
        pe_bT = sem("pe_bT")
        vec_bT = sem("vec_bT")
        pe_pair = sem("pe_pair")
        vec_pair = sem("vec_pair")
        act_pair = sem("act_pair")
        vec_conv = sem("vec_conv")
        act_silu = sem("act_silu")
        pe_ba = sem("pe_ba")
        vec_ba = sem("vec_ba")
        act_ba = sem("act_ba")
        vec_pooled = sem("vec_pooled")
        pe_ypool = sem("pe_ypool")
        vec_ypool = sem("vec_ypool")
        pool_sq = sem("pool_sq")
        pe_ssq = sem("pe_ssq")
        act_norm = sem("act_norm")
        vec_norm = sem("vec_norm")
        vec_g = sem("vec_g")
        pe_g = sem("pe_g")

        vec_diag = sem("vec_diag")
        pe_grow = sem("pe_grow")
        pe_kk = sem("pe_kk")
        vec_darg = sem("vec_darg")
        act_decay = sem("act_decay")
        pool_decay = sem("pool_decay")
        vec_l = sem("vec_l")
        pe_nat = sem("pe_nat")
        vec_nat = sem("vec_nat")
        pe_lT = sem("pe_lT")
        vec_lT = sem("vec_lT")
        pool_off = sem("pool_off")
        vec_inv = sem("vec_inv")
        pe_prod = sem("pe_prod")
        act_prod = sem("act_prod")
        pe_corr = sem("pe_corr")
        pe_uw = sem("pe_uw")
        act_u = sem("act_u")
        vec_w = sem("vec_w")
        pe_ws = sem("pe_ws")
        vec_vnew = sem("vec_vnew")
        pe_o = sem("pe_o")
        vec_state = sem("vec_state")
        vec_o = sem("vec_o")
        pe_z = sem("pe_z")
        act_z = sem("act_z")
        pool_osq = sem("pool_osq")
        vec_ossq = sem("vec_ossq")
        act_orms = sem("act_orms")
        vec_on = sem("vec_on")
        act_zs = sem("act_zs")
        pe_oT = sem("pe_oT")
        vec_yg = sem("vec_yg")
        pe_ada2 = sem("pe_ada2")
        vec_mod2 = sem("vec_mod2")
        pe_tail = sem("pe_tail")
        act_gate1 = sem("act_gate1")
        vec_tail = sem("vec_tail")
        pe_mo = sem("pe_mo")
        vec_x1 = sem("vec_x1")
        act_x1sq = sem("act_x1sq")
        vec_xn2 = sem("vec_xn2")
        pe_h2T = sem("pe_h2T")
        vec_h2T = sem("vec_h2T")
        pe_h2 = sem("pe_h2")
        act_h2 = sem("act_h2")
        pe_logits = sem("pe_logits")
        vec_logits = sem("vec_logits")
        act_top = sem("act_top")
        vec_mask = sem("vec_mask")
        pe_rank = sem("pe_rank")
        vec_route = sem("vec_route")

        vec_sel = sem("vec_sel")
        pe_gather = sem("pe_gather")
        vec_xT = sem("vec_xT")
        act_xT = sem("act_xT")
        vec_hu = sem("vec_hu")
        act_sig = sem("act_sig")
        vec_act = sem("vec_act")
        pe_selT = sem("pe_selT")
        act_selT = sem("act_selT")
        act_yT = sem("act_yT")
        pe_yn = sem("pe_yn")
        vec_yn = sem("vec_yn")
        act_yn = sem("act_yn")
        moe_chain = sem("moe_chain")
        pe_moe = sem("pe_moe")
        act_fin = sem("act_fin")
        vec_fin = sem("vec_fin")
        vec_out = sem("vec_out")

        def cut(w, lo, n=CW):
            return w[0, :, lo:lo + n].rearrange("(c p) n -> p c n", p=P)

        def slot_as(i, c):
            return ring[:, i, :, :].rearrange("p c n -> p (c n)").rearrange("p (c n) -> p c n", c=c)

        chunks = [("ada", cut(ada_w, CW * i)) for i in range(4)]
        chunks += [("qkv", cut(w_in, COL_QKV + CW * i)) for i in range(6)]
        chunks += [("pool", cut(w_in, COL_POOL))]
        chunks += [("gate0", cut(w_in, COL_GATE + CW * i)) for i in range(2)]
        chunks += [("pool_out", w_pool_out[0].rearrange("(c p) n -> p c n", p=P))]
        chunks += [("z", cut(w_in, COL_Z + CW * i)) for i in range(2)]
        chunks += [("ada2", cut(ada_w, CW * i)) for i in range(4, 12)]
        chunks += [("gate1", cut(w_in, COL_GATE + D + CW * i)) for i in range(2)]
        chunks += [("gdn_out", cut(w_gdn_out, CW * i)) for i in range(2)]
        chunks += [("w_out", cut(w_out, CW * i)) for i in range(2)]
        first = {}
        for n, (kind, _) in enumerate(chunks):
            first.setdefault(kind, n)
        USES = len(chunks) // RING
        assert len(chunks) % RING == 0

        w1_dram = exp_w1.rearrange("l e (c p) n -> (l e) p c n", p=P)
        w2_dram = exp_w2.rearrange("l e (c p) n -> (l e) p c n", p=P)

        def w_slot(n, j, k):
            return ring[:, n % RING, k, j * P:(j + 1) * P]

        block = ctx.enter_context(nc.Block())

        def rounds(eng, body):
            body(0)
            eng.wait_ge(vec_route, 1)
            n = eng.value_load(rounds_i[0:1, 0:1], min_val=1, max_val=ROUNDS)
            with eng.Fori(1, ROUNDS) as r:
                with eng.If(r < n):
                    body(r)

        @block.sync
        def _(sp):
            sp.dma_start(rows[ROW_C:ROW_C + 8, :], c.rearrange("b (r n) -> (b r) n", n=P)).then_inc(rows_in, 16)
            sp.dma_start(rows[ROW_ADA_B:ROW_ADA_B + 48, :],
                         ada_b.rearrange("l (r n) -> (l r) n", n=P)).then_inc(rows_in, 16)
            sp.dma_start(consts[:, :], const).then_inc(const_in, 16)
            for t in range(T):
                sp.dma_start(xt[:, t, :], x[0, t * P:(t + 1) * P, :]).then_inc(x_in, 16)
            for n, (kind, src) in enumerate(chunks):
                if n >= RING:
                    sp.wait_ge(used[n % RING], n // RING)
                dst = slot_as(n % RING, 4) if kind == "pool_out" else ring[:, n % RING, :, :]
                sp.dma_start(dst, src).then_inc(landed[n % RING], 16)

            def stream(r):
                with sp.Fori(0, E) as e:
                    for s in range(RING):
                        src = w1_dram[e, :, :, s * CW:(s + 1) * CW] if s < 4 else \
                            w2_dram[e, :, :, (s - 4) * CW:(s - 3) * CW]
                        sp.wait_ge(used[s], r * E + e + USES)
                        sp.dma_start(ring[:, s, :, :], src).then_inc(landed[s], 16)

            rounds(sp, stream)
            for t in range(T):
                sp.wait_ge(vec_out, t + 1)
                sp.dma_start(out[0, t * P:(t + 1) * P, :], fin[:, t, :]).then_inc(out_done, 16)
            sp.wait_ge(out_done, 16 * T)

        @block.gpsimd
        def _(pool):
            chain = [0]

            def link(ins):
                chain[0] += 1
                ins.then_inc(pool_chain, 1)
                pool.wait_ge(pool_chain, chain[0])

            pool.dma_start(pw, pool_w[0].rearrange("g p n -> p g n")).then_inc(early_in, 16)
            pool.dma_start(wba, cut(w_in, COL_BA, 2 * HEADS)).then_inc(early_in, 16)
            pool.dma_start(small[:, 0:8], dt_bias[0].partition_broadcast(P)).then_inc(early_in, 16)
            pool.dma_start(small[:, 8:16], a_log[0].partition_broadcast(P)).then_inc(early_in, 16)
            pool.dma_start(rb[:, :], router_b[0].partition_broadcast(P)).then_inc(early_in, 16)
            pool.dma_start(rw[:, :, :], router_w[0].rearrange("(c p) n -> p c n", p=P)).then_inc(early_in, 16)

            for i in range(8):
                pool.wait_ge(act_silu, i + 1)
                if i == 0:
                    pool.wait_ge(vec_bT, 1)
                src = qkv[:, 2 * i:2 * i + 2, :].rearrange("p a s -> p (a s)")
                nc.gpsimd.tensor_tensor(sq[:, i, :], src, src, ALU.mult).then_inc(pool_sq, 1)

            for g in range(2):
                for t in range(T):
                    b = 2 * g + t
                    pool.wait_ge(act_decay, b + 1)
                    nc.gpsimd.tensor_tensor(decay[:, t], decay[:, t], over_heads(const_tile("strict")), ALU.mult)
                    nc.gpsimd.tensor_tensor(decayT[:, t], decayT[:, t], over_heads(const_tile("causal")),
                                            ALU.mult).then_inc(pool_decay, 1)
                for t in range(T):
                    b = 2 * g + t
                    pool.wait_ge(vec_l, b + 1)
                    nc.gpsimd.tensor_tensor(inv[:, t], decay[:, t], over_heads(const_tile("off1")),
                                            ALU.mult).then_inc(pool_off, 1)
                    pool.wait_ge(vec_lT, b + 1)
                    nc.gpsimd.tensor_tensor(invT[:, t], lT[:, t], over_heads(const_tile("off1T")),
                                            ALU.mult).then_inc(pool_off, 1)
                for i, s in enumerate((2, 4, 8, 16, 32)):
                    for t in range(T):
                        if i:
                            pool.wait_ge(pe_prod, 10 * g + 2 * (i - 1) + t + 1)
                        nc.gpsimd.tensor_tensor(off[:, t], lT[:, t], over_heads(const_tile(f"off{s}T")),
                                                ALU.mult).then_inc(pool_off, 1)
            pool.wait_ge(vec_o, 4)
            pool.wait_ge(vec_state, 6)
            pool.dma_start(fin_g, final_norm_g.partition_broadcast(P)).then_inc(fin_in, 16)
            nc.gpsimd.tensor_tensor(o_sq, v_of.rearrange("p h s -> p (h s)"), v_of.rearrange("p h s -> p (h s)"),
                                    ALU.mult).then_inc(pool_osq, 1)

        @block.scalar
        def _(act):
            chain = [0]

            def link(ins):
                chain[0] += 1
                ins.then_inc(act_chain, 1)
                act.wait_ge(act_chain, chain[0])

            for j in range(TAPS):
                act.dma_start(conv_rows[24 * j:24 * j + 24, :],
                              conv_w[0, j, :].rearrange("(r n) -> r n", n=P)).then_inc(rows_in, 16)
            for row, src, n in ((ROW_G1, norm_mix_g, 8), (ROW_G2, norm_ffn_g, 8), (ROW_POOL, pool_scale, 4),
                                (ROW_GDN, gdn_norm_g, 1)):
                act.dma_start(rows[row:row + n, :], src.rearrange("l (r n) -> (l r) n", n=P)).then_inc(rows_in, 16)
            act.dma_start(b1_rows[0:E, :], exp_b1[0]).then_inc(b_in, 16)
            act.dma_start(b2_rows[0:E, :], exp_b2[0]).then_inc(b_in, 16)

            act.wait_ge(vec_cols, 1)
            nc.scalar.activation(c_act[:, :], cols[:, ROW_C:ROW_C + 8], ACT.Silu).then_inc(act_c, 1)
            act.wait_ge(x_in, 16 * T)
            for t in range(T):
                nc.scalar.activation(region_y[:, 4 * t:4 * t + 4, :].rearrange("p c s -> p (c s)"), xt[:, t, :],
                                     ACT.Square, accum_out=stat[:, 0, t:t + 1]).then_inc(act_xsq, 1)
            act.wait_ge(act_xsq, 2)
            act.wait_ge(vec_cols, 2)
            nc.scalar.activation(stat[:, 0, 2:4], stat[:, 0, 0:2], ACT.Sqrt, scale=1.0 / D,
                                 bias=small[:, 16:17]).then_inc(act_xrms, 1)
            for i in range(12):
                act.wait_ge(vec_conv, i + 1)
                a = qkv[:, 2 * i:2 * i + 2, :]
                nc.scalar.activation(a, a, ACT.Silu).then_inc(act_silu, 1)
            act.wait_ge(pe_ba, 1)
            act.wait_ge(vec_ba, 1)
            nc.scalar.activation(heads_in[:, BETA], bank[4][:, 0:32].rearrange("p (t n) -> p t n", t=T)[:, :, 0:8],
                                 ACT.Sigmoid).then_inc(act_ba, 1)
            for i in range(4):
                act.wait_ge(pe_pair, 14 + i + 1)
                nc.scalar.activation(region_y[:, 2 * i:2 * i + 2, :], pair((14 + i) % 4),
                                     ACT.Sigmoid).then_inc(act_pair, 1)
            act.wait_ge(vec_ba, 2)
            nc.scalar.activation(heads_in[:, EMAG], heads_in[:, MAG], ACT.Exp, scale=-1.0)
            nc.scalar.activation(small[:, 24:32], small[:, 8:16], ACT.Exp).then_inc(act_ba, 1)
            for i in range(8):
                act.wait_ge(pe_ssq, i + 1)
                if i < 4:
                    op = nc.scalar.activation(sq[:, i, :], bank[4 + i % 2][:, :], ACT.Sqrt, scale=float(P),
                                              bias=small[:, 17:18])
                else:
                    op = nc.scalar.activation(sq[:, i, :], bank[4 + i % 2][:, :], ACT.Sqrt, bias=small[:, 16:17])
                op.then_inc(act_norm, 1)
            act.wait_ge(vec_g, 3)
            nc.scalar.activation(heads_in[:, EG], heads_in[:, GC], ACT.Exp)
            nc.scalar.activation(heads_in[:, KDF], heads_in[:, KDF], ACT.Exp).then_inc(act_ba, 1)

            def z_copy(i):
                act.wait_ge(pe_z, i + 1)
                nc.scalar.activation(region_z[:, 2 * i:2 * i + 2, :], pair(7), ACT.Copy).then_inc(act_z, 1)

            for g in range(2):
                for t in range(T):
                    b = 2 * g + t
                    act.wait_ge(vec_darg, b + 1)
                    nc.scalar.activation(eg_row[:, t], quad(3 * t), ACT.Exp)
                    nc.scalar.activation(decay[:, t], decay[:, t], ACT.Exp, scale=-1.0)
                    nc.scalar.activation(decayT[:, t], decayT[:, t], ACT.Exp).then_inc(act_decay, 1)
                z_copy(2 * g)
                z_copy(2 * g + 1)
                for i in range(5):
                    for t in range(T):
                        act.wait_ge(pe_prod, 10 * g + 2 * i + t + 1)
                        nc.scalar.activation(prod[:, t], quad(3 * t + 1), ACT.Copy).then_inc(act_prod, 1)
                for t in range(T):
                    act.wait_ge(pe_uw, 2 * g + t + 1)
                    nc.scalar.activation(vb[:, t], quad(3 * t), ACT.Copy).then_inc(act_u, 1)
            act.wait_ge(pe_o, 8)
            act.wait_ge(vec_ossq, 1)
            for t in range(T):
                act.dma_start(xt[:, t, :], x[0, t * P:(t + 1) * P, :]).then_inc(x_in, 16)
            nc.scalar.activation(small[:, 32:48], small[:, 32:48], ACT.Sqrt, scale=1.0 / P,
                                 bias=small[:, 16:17]).then_inc(act_orms, 1)
            act.wait_ge(act_z, 4)
            nc.scalar.activation(region_z[:, :, :], region_z[:, :, :], ACT.Silu).then_inc(act_zs, 1)
            for i in range(4):
                act.wait_ge(pe_tail, i + 1)
                nc.scalar.activation(gate1[:, 2 * i:2 * i + 2, :], pair(4 + i), ACT.Sigmoid).then_inc(act_gate1, 1)
            act.wait_ge(vec_x1, 4)
            for t in range(T):
                nc.scalar.activation(moT[:, 4 * t:4 * t + 4, :].rearrange("p h s -> p (h s)"), xt[:, t, :],
                                     ACT.Square, accum_out=stat[:, 1, t:t + 1]).then_inc(act_x1sq, 1)
            act.wait_ge(act_x1sq, 2)
            nc.scalar.activation(stat[:, 1, 2:4], stat[:, 1, 0:2], ACT.Sqrt, scale=1.0 / D,
                                 bias=small[:, 16:17]).then_inc(act_x1sq, 1)
            for i in range(4):
                act.wait_ge(pe_h2, i + 1)
                nc.scalar.activation(h2[:, i // 2, (i % 2) * 512:(i % 2 + 1) * 512], bank[i][:, :],
                                     ACT.Copy).then_inc(act_h2, 1)
            act.wait_ge(vec_logits, 1)
            nc.scalar.activation(expw[:, :, 0:4], expw[:, :, 0:4], ACT.Exp).then_inc(act_top, 1)

            def moe(r):
                n0 = r * E

                def body(n, e, prologue=False, scatter=True):
                    act.wait_ge(vec_hu, 4 * n + 1)
                    nc.scalar.activation(sig[:, :, :], hu[:, 0:2, :], ACT.Sigmoid, scale=ALPHA).then_inc(act_sig, 1)
                    if scatter:
                        y_rows(n)
                    for j in range(1, 4):
                        act.wait_ge(vec_hu, 4 * n + j + 1)
                        nc.scalar.activation(sig[:, :, :], hu[:, 0:2, :], ACT.Sigmoid,
                                             scale=ALPHA).then_inc(act_sig, 1)
                    x_cols(n + r + 2)
                    act.wait_ge(pe_selT, n + 1)
                    nc.scalar.activation(wselT, bank[0][0:SLOTS, 0:T * P], ACT.Copy).then_inc(act_selT, 1)
                    for half in range(2):
                        act.wait_ge(used[4 + half], n + USES + 1)
                        for j in range(4):
                            f = 4 * half + j
                            op = nc.scalar.activation(yT[:, f, :], bank[1 + half][:, j * SLOTS:(j + 1) * SLOTS],
                                                      ACT.Identity, scale=mod[:, 40 + f:41 + f],
                                                      bias=b2_cols[:, f, bass.ds(e, 1)])
                    op.then_inc(act_yT, 1)

                def x_cols(count):
                    act.wait_ge(pe_gather, count)
                    nc.scalar.activation(xT[:, 4:8, :], bank[3][:, 0:4 * SLOTS], ACT.Copy).then_inc(act_xT, 1)

                def y_rows(n):
                    act.wait_ge(pe_yn, n)
                    nc.scalar.activation(y_nat[:, 512:1024], bank[3][0:SLOTS, :], ACT.Copy).then_inc(act_yn, 1)

                x_cols(n0 + r + 1)
                body(n0, 0, scatter=False)
                with act.Fori(1, E) as e:
                    body(n0 + e, e)
                y_rows(n0 + E)

            rounds(act, moe)
            act.wait_ge(pe_moe, 1)
            for i in range(4):
                nc.scalar.activation(fin[:, i // 2, (i % 2) * 512:(i % 2 + 1) * 512], bank[4 + i][:, :], ACT.Square,
                                     accum_out=stat[:, 0, i:i + 1]).then_inc(act_fin, 1)
            act.wait_ge(vec_fin, 1)
            nc.scalar.activation(stat[:, 1, 0:2], stat[:, 1, 0:2], ACT.Sqrt, scale=1.0 / D,
                                 bias=small[:, 16:17]).then_inc(act_fin, 1)

        @block.tensor
        def _(pe):
            def arrived(n):
                pe.wait_ge(landed[n % RING], 16 * (n // RING + 1))

            done_chunk = []

            def free_slot(n):
                done_chunk.append(n)

            def carry(mm):
                if done_chunk:
                    mm.then_inc(used[done_chunk.pop() % RING], 1)

            def project(out_ap, n, j, rhs, kc=KC, w=None):
                for k in range(kc):
                    mm = nc.tensor.matmul(out_ap, w(k) if w else w_slot(n, j, k), rhs[:, k, :],
                                          start=(k == 0), stop=(k == kc - 1))
                    if k == 0:
                        carry(mm)
                return mm

            pe.wait_ge(const_in, 16)
            pe.wait_ge(rows_in, 16 * 10)
            nc.tensor.transpose(bank[6][:, 0:ROWS], rows[0:ROWS, :], ident[0:ROWS, 0:ROWS])
            nc.tensor.transpose(bank[6][:, 128:128 + 96], conv_rows[0:96, :], ident[0:96, 0:96]).then_inc(pe_rows, 1)
            pe.wait_ge(vec_xn, 2)
            for f in range(KC):
                for t in range(T):
                    mm = nc.tensor.transpose(pair(f // 2)[:, f % 2, t * P:(t + 1) * P],
                                             xt[:, t, f * P:(f + 1) * P], ident)
            mm.then_inc(pe_xT, 1)
            pe.wait_ge(b_in, 32)
            for j in range(4):
                for a in range(4):
                    lo = CW * j + 2 * P * (a % 2) + a // 2
                    nc.tensor.transpose(bank[7][:, (4 * j + a) * E:(4 * j + a + 1) * E],
                                        b1_rows[0:E, lo:lo + 2 * P - 1:2], ident[0:E, 0:E])
            for f in range(KC):
                mm = nc.tensor.transpose(bank[4][:, f * E:(f + 1) * E], b2_rows[0:E, f * P:(f + 1) * P],
                                         ident[0:E, 0:E])
            mm.then_inc(pe_bT, 1)
            pe.wait_ge(act_c, 1)

            def ada_column(n, j, out_ap):
                for k in range(KC):
                    mm = nc.tensor.matmul(out_ap, w_slot(n, j, k), c_act[:, k:k + 1],
                                          start=(k == 0), stop=(k == KC - 1))
                    if k == 0:
                        carry(mm)
                return mm

            for n in range(4):
                arrived(n)
                for j in range(4):
                    col = 4 * n + j
                    mm = ada_column(n, j, bank[5][:, col:col + 1])
                free_slot(n)
            mm.then_inc(pe_ada, 1)
            pe.wait_ge(vec_hT, 1)
            released = {}
            for i in range(12):
                released[i] = (vec_conv, i + 1)
            for i in range(2):
                released[12 + i] = (vec_pair, i + 1)
            for i in range(4):
                released[14 + i] = (act_pair, i + 1)

            def pair_of(i, n, j, rhs, kc=KC, w=None):
                if i >= 4:
                    pe.wait_ge(*released[i - 4])
                for a in range(2):
                    mm = project(pair(i % 4)[:, a, :], n, j + a, rhs, kc, w and (lambda k, a=a: w(k, a)))
                mm.then_inc(pe_pair, 1)
                return mm

            for i in range(12):
                n = first["qkv"] + i // 2
                arrived(n)
                pair_of(i, n, 2 * (i % 2), hT)
                if i % 2:
                    free_slot(n)
            pe.wait_ge(early_in, 16 * 6)
            pe.wait_ge(vec_bT, 1)
            for t in range(T):
                for k in range(KC):
                    mm = nc.tensor.matmul(bank[4][:, t * 16:(t + 1) * 16], hT[:, k, t * P:(t + 1) * P], wba[:, k, :],
                                          start=(k == 0), stop=(k == KC - 1))
            mm.then_inc(pe_ba, 1)
            arrived(first["pool"])
            for i in range(2):
                pair_of(12 + i, first["pool"], 2 * i, hT)
            free_slot(first["pool"])
            for i in range(4):
                n = first["gate0"] + i // 2
                arrived(n)
                pair_of(14 + i, n, 2 * (i % 2), hT)
                if i % 2:
                    free_slot(n)
            pe.wait_ge(vec_g, 1)
            nc.tensor.matmul(bank[6][:, 0:16], const_tile("causal"), heads_in[:, G].rearrange("p t h -> p (t h)"),
                             start=True, stop=True).then_inc(pe_g, 1)
            pe.wait_ge(vec_pooled, 1)
            pe.wait_ge(act_ba, 1)
            for i in range(2):
                for a in range(2):
                    mm = nc.tensor.matmul(pair(4 + i)[:, a, :], pw[:, 2 * i + a, :], pool_b[:, 2 * i + a, :],
                                          start=True, stop=True)
            mm.then_inc(pe_ypool, 1)
            pe.wait_ge(vec_g, 2)
            nc.tensor.matmul(bank[6][:, 0:16], const_tile("after"), heads_in[:, G].rearrange("p t h -> p (t h)"),
                             start=True, stop=True).then_inc(pe_g, 1)
            pe.wait_ge(vec_ypool, 1)
            for i in range(8):
                pe.wait_ge(pool_sq, i + 1)
                if i >= 2:
                    pe.wait_ge(act_norm, i - 1)
                nc.tensor.matmul(bank[4 + i % 2][:, :], ones, sq[:, i, :], start=True, stop=True).then_inc(pe_ssq, 1)
            n = first["pool_out"]
            arrived(n)
            wp = slot_as(n % RING, 4)
            for i in range(4):
                pair_of(18 + i, n, 0, y_pool, 4, lambda k, a, i=i: wp[:, k, (2 * i + a) * P:(2 * i + a + 1) * P])
            free_slot(n)

            def z_pair(i):
                n = first["z"] + i // 2
                arrived(n)
                if i:
                    pe.wait_ge(act_z, i)
                for a in range(2):
                    mm = project(pair(7)[:, a, :], n, 2 * (i % 2) + a, hT)
                mm.then_inc(pe_z, 1)
                if i % 2:
                    free_slot(n)

            ada2 = [0]

            def ada2_columns(count):
                for _ in range(count):
                    col = ada2[0]
                    n = first["ada2"] + col // 4
                    if col % 4 == 0:
                        arrived(n)
                    mm = ada_column(n, col % 4, bank[6][:, col:col + 1])
                    if col % 4 == 3:
                        free_slot(n)
                    ada2[0] += 1
                return mm

            pe.wait_ge(vec_pair, 6)
            for g in range(2):
                hs = [HG * g + h for h in range(HG)]
                for t in range(T):
                    b = 2 * g + t
                    tok = slice(t * P, (t + 1) * P)
                    if g:
                        pe.wait_ge(vec_o, 2 * g - 1 + t)
                        pe.wait_ge(vec_state, 3 * g)
                    pe.wait_ge(vec_norm, 8)
                    for h in hs:
                        nc.tensor.matmul(quad(3 * t + 1)[:, h % HG], k_of[:, h, tok], k_of[:, h, tok],
                                         start=True, stop=True)
                    for h in hs:
                        mm = nc.tensor.matmul(quad(3 * t + 2)[:, h % HG], k_of[:, h, tok], q_of[:, h, tok],
                                              start=True, stop=True)
                    mm.then_inc(pe_kk, 1)
                    pe.wait_ge(vec_diag, b + 1)
                    nc.tensor.matmul(bank[3 * t][:, :], ones, prod[:, t].rearrange("p h n -> p (h n)"),
                                     start=True, stop=True).then_inc(pe_grow, 1)
                z_pair(2 * g)
                z_pair(2 * g + 1)
                for t in range(T):
                    b = 2 * g + t
                    tok = slice(t * P, (t + 1) * P)
                    pe.wait_ge(vec_l, b + 1)
                    for h in hs:
                        nc.tensor.transpose(quad(3 * t + 1)[:, h % HG], k_of[:, h, tok], ident)
                    for h in hs:
                        mm = nc.tensor.transpose(quad(3 * t + 2)[:, h % HG], v_of[:, h, tok], ident)
                    mm.then_inc(pe_nat, 1)
                    for h in hs:
                        mm = nc.tensor.transpose(quad(3 * t)[:, h % HG], decay[:, t, h % HG], ident)
                    mm.then_inc(pe_lT, 1)
                for i in range(5):
                    for t in range(T):
                        pe.wait_ge(pool_off, 14 * g + 4 + 2 * i + t + 1)
                        pe.wait_ge(vec_inv, 12 * g + 2 * i + t + 1)
                        if i == 0:
                            pe.wait_ge(vec_nat, 2 * g + t + 1)
                        for h in range(HG):
                            mm = nc.tensor.matmul(quad(3 * t + 1)[:, h], off[:, t, h], inv[:, t, h],
                                                  start=True, stop=True)
                        mm.then_inc(pe_prod, 1)
                    for t in range(T):
                        pe.wait_ge(act_prod, 10 * g + 2 * i + t + 1)
                        if i < 4:
                            for h in range(HG):
                                nc.tensor.matmul(quad(3 * t)[:, h], invT[:, t, h], prod[:, t, h],
                                                 start=True, stop=True)
                        for h in range(HG):
                            mm = nc.tensor.matmul(quad(3 * t + 2)[:, h], prod[:, t, h], invT[:, t, h],
                                                  start=True, stop=True)
                        mm.then_inc(pe_corr, 1)
                for t in range(T):
                    pe.wait_ge(vec_inv, 12 * g + 10 + t + 1)
                    for h in range(HG):
                        nc.tensor.matmul(quad(3 * t)[:, h], invT[:, t, h], vb[:, t, h], start=True, stop=True)
                    for h in range(HG):
                        mm = nc.tensor.matmul(quad(3 * t + 1)[:, h], kbg[:, t, h], invT[:, t, h],
                                              start=True, stop=True)
                    mm.then_inc(pe_uw, 1)
                for ci in range(S // CHUNK):
                    t, lo = ci // 2, CHUNK * (ci % 2)
                    rows_c = slice(lo, lo + CHUNK)
                    tok = slice(t * P + lo, t * P + lo + CHUNK)
                    if ci % 2 == 0:
                        pe.wait_ge(act_u, 2 * g + t + 1)
                        pe.wait_ge(vec_w, 2 * g + t + 1)
                    if ci:
                        pe.wait_ge(vec_state, 3 * g + ci)
                        for h in range(HG):
                            mm = nc.tensor.matmul(quad(3 * t)[rows_c, h], kbg[:, t, h, rows_c], state[:, h],
                                                  start=True, stop=True)
                        mm.then_inc(pe_ws, 1)
                    ada2_columns(2)
                    if ci:
                        pe.wait_ge(vec_vnew, 3 * g + ci)
                    for h in range(HG):
                        if ci:
                            nc.tensor.matmul(quad(3 * t + 1)[rows_c, h], q_of[:, HG * g + h, tok], state[:, h],
                                             start=True, stop=False)
                        mm = nc.tensor.matmul(quad(3 * t + 1)[rows_c, h], decayT[rows_c, t, h, rows_c],
                                              vb[rows_c, t, h], start=(ci == 0), stop=True)
                    if ci < S // CHUNK - 1:
                        for h in range(HG):
                            mm = nc.tensor.matmul(quad(3 * t + 2)[:, h], kdec[rows_c, t, h], vb[rows_c, t, h],
                                                  start=True, stop=True)
                    mm.then_inc(pe_o, 1)
                    mm = ada2_columns(2)
            mm.then_inc(pe_ada2, 1)

            def tail_pair(i, n, b, rhs):
                for a in range(2):
                    mm = project(pair(b)[:, a, :], n, 2 * (i % 2) + a, rhs)
                mm.then_inc(pe_tail, 1)
                if i % 2:
                    free_slot(n)

            pe.wait_ge(vec_mod2, 1)
            pe.wait_ge(vec_o, 4)
            pe.wait_ge(vec_state, 6)
            for i in range(4):
                n = first["gate1"] + i // 2
                arrived(n)
                tail_pair(i, n, 4 + i, hT)
            pe.wait_ge(vec_on, 1)
            for h in range(HEADS):
                for t in range(T):
                    mm = nc.tensor.transpose(pair(h // 2)[:, h % 2, t * P:(t + 1) * P],
                                             o_nat[:, h // HG, t, h % HG], ident)
            mm.then_inc(pe_oT, 1)
            pe.wait_ge(vec_yg, 4)
            for i in range(4):
                n = first["gdn_out"] + i // 2
                arrived(n)
                tail_pair(i, n, i, region_z)
            pe.wait_ge(act_gate1, 4)
            pe.wait_ge(vec_tail, 4)
            for i in range(4):
                n = first["w_out"] + i // 2
                arrived(n)
                tail_pair(i, n, 4 + i, region_y)
            pe.wait_ge(vec_tail, 8)
            for t in range(T):
                for half in range(2):
                    for j in range(4):
                        f = 4 * half + j
                        mm = nc.tensor.transpose(bank[2 * t + half][:, j * P:(j + 1) * P],
                                                 moT[:, f, t * P:(t + 1) * P], ident)
                        if j == 0:
                            carry(mm)
                    mm.then_inc(pe_mo, 1)
            pe.wait_ge(vec_xn2, 2)
            for f in range(KC):
                for t in range(T):
                    mm = nc.tensor.transpose(pair(4 + f // 2)[:, f % 2, t * P:(t + 1) * P],
                                             xn2[:, t, f * P:(f + 1) * P], ident)
                if f % 2:
                    mm.then_inc(pe_h2T, 1)
            pe.wait_ge(vec_h2T, 1)
            for t in range(T):
                for half in range(2):
                    for j in range(4):
                        f = 4 * half + j
                        mm = nc.tensor.transpose(bank[2 * t + half][:, j * P:(j + 1) * P],
                                                 h2T[:, f, t * P:(t + 1) * P], ident)
                    mm.then_inc(pe_h2, 1)
            for t in range(T):
                for k in range(KC):
                    mm = nc.tensor.matmul(bank[4][:, t * E:(t + 1) * E], h2T[:, k, t * P:(t + 1) * P], rw[:, k, :],
                                          start=(k == 0), stop=(k == KC - 1))
            mm.then_inc(pe_logits, 1)
            pe.wait_ge(vec_mask, 1)
            for t in range(T):
                nc.tensor.matmul(bank[5][:, t * E:(t + 1) * E], const_tile("before"), mask[:, t, :],
                                 start=True, stop=(t == 0))
                if t:
                    nc.tensor.matmul(bank[5][:, t * E:(t + 1) * E], ones, mask[:, 0, :], start=False, stop=True)
            for t in range(T):
                mm = nc.tensor.matmul(bank[5][:, 2 * E:3 * E], ones, mask[:, t, :], start=(t == 0), stop=(t == 1))
            mm.then_inc(pe_rank, 1)
            pe.wait_ge(vec_route, 1)
            pe.wait_ge(act_h2, 4)
            for t in range(T):
                for half in range(2):
                    nc.tensor.matmul(bank[4 + 2 * t + half][:, :], ident, xt[:, t, half * 512:(half + 1) * 512],
                                     start=True, stop=False, skip_group_check=True)

            def moe(r):
                n0 = r * E

                def w1_chunk(n, j):
                    pe.wait_ge(landed[j], 16 * (n + USES + 1))
                    for a in range(4):
                        lo = 2 * P * (a % 2) + a // 2
                        for k in range(KC):
                            mm = nc.tensor.matmul(bank[j % 2][:, a * SLOTS:(a + 1) * SLOTS],
                                                  ring[:, j, k, lo:lo + 2 * P - 1:2], xT[:, k, :],
                                                  start=(k == 0), stop=(k == KC - 1))
                    return mm

                def w2_chunk(n, j):
                    pe.wait_ge(landed[4 + j], 16 * (n + USES + 1))
                    for a in range(4):
                        for k in range(KC):
                            mm = nc.tensor.matmul(bank[1 + j][:, a * SLOTS:(a + 1) * SLOTS],
                                                  ring[:, 4 + j, k, a * P:(a + 1) * P], actT[:, k, :],
                                                  start=(k == 0), stop=(k == KC - 1))
                    return mm

                def gather(count):
                    pe.wait_ge(vec_sel, count)
                    for f in range(KC):
                        for t in range(T):
                            mm = nc.tensor.matmul(bank[2 + f // 4][:, f % 4 * SLOTS:(f % 4 + 1) * SLOTS],
                                                  h2[:, t, f * P:(f + 1) * P], sel[:, t, :],
                                                  start=(t == 0), stop=(t == T - 1))
                    mm.then_inc(pe_gather, 1)

                def turn_y(n):
                    pe.wait_ge(act_yT, n)
                    for f in range(KC):
                        mm = nc.tensor.transpose(bank[2 + f // 4][0:SLOTS, f % 4 * P:(f % 4 + 1) * P],
                                                 yT[:, f, :], ident)
                    mm.then_inc(pe_yn, 1)

                def scatter(n):
                    pe.wait_ge(vec_yn, n)
                    pe.wait_ge(act_yn, n)
                    for t in range(T):
                        for half in range(2):
                            nc.tensor.matmul(bank[4 + 2 * t + half][:, :], wselT[:, t * P:(t + 1) * P],
                                             y_nat[:, half * 512:(half + 1) * 512],
                                             start=False, stop=False, skip_group_check=True)

                def body(n, first_expert=False):
                    pe.wait_ge(vec_xT, n + r + 1)
                    pe.wait_ge(act_xT, n + r + 1)
                    if not first_expert:
                        pe.wait_ge(act_selT, n)
                    w1_chunk(n, 0).then_inc(used[0], 1)
                    if not first_expert:
                        turn_y(n)
                    w1_chunk(n, 1).then_inc(used[1], 1)
                    if not first_expert:
                        scatter(n)
                    for j in range(2, 4):
                        pe.wait_ge(vec_hu, 4 * n + j - 1)
                        w1_chunk(n, j).then_inc(used[j], 1)
                    gather(n + r + 2)
                    pe.wait_ge(vec_hu, 4 * n + 3)
                    for t in range(T):
                        mm = nc.tensor.transpose(bank[0][0:SLOTS, t * P:(t + 1) * P], wsel[:, t, :], ident)
                    mm.then_inc(pe_selT, 1)
                    pe.wait_ge(vec_act, 4 * n + 4)
                    w2_chunk(n, 0).then_inc(used[4], 1)
                    pe.wait_ge(vec_xT, n + r + 2)
                    w2_chunk(n, 1).then_inc(used[5], 1)

                gather(n0 + r + 1)
                body(n0, first_expert=True)
                with pe.Fori(1, E) as e:
                    body(n0 + e)
                turn_y(n0 + E)
                scatter(n0 + E)

            rounds(pe, moe)
            for i in range(4):
                mm = nc.tensor.matmul(bank[4 + i][:, 0:1], const_tile("before")[:, 0:P], const_tile("strict")[:, 127:128],
                                      start=False, stop=True, skip_group_check=True)
            mm.then_inc(pe_moe, 1)

        @block.vector
        def _(dve):
            chain = [0]

            def link(*steps):
                for ins in steps:
                    chain[0] += 1
                    ins.then_inc(vec_chain, 1)
                dve.wait_ge(vec_chain, chain[0])

            tt, ts, stt = nc.vector.tensor_tensor, nc.vector.tensor_scalar, nc.vector.scalar_tensor_tensor
            copy, recip = nc.vector.tensor_copy, nc.vector.reciprocal

            link(nc.vector.memset(small[:, 16:17], EPS), nc.vector.memset(small[:, 17:18], EPS * P))
            dve.wait_ge(pe_rows, 1)
            copy(cols[:, :], bank[6][:, 0:ROWS]).then_inc(vec_cols, 1)
            copy(conv_cols[:, :, :], bank[6][:, 128:128 + 96].rearrange("p (j b) -> p j b", j=TAPS)).then_inc(vec_cols, 1)
            dve.wait_ge(vec_cols, 2)
            dve.wait_ge(act_xrms, 1)
            link(recip(stat[:, 0, 2:4], stat[:, 0, 2:4]))
            for t in range(T):
                ts(xt[:, t, :], xt[:, t, :], stat[:, 0, 2 + t:3 + t], None, ALU.mult).then_inc(vec_xn, 1)
            dve.wait_ge(pe_bT, 1)
            copy(b1_cols[:, :, :, :].rearrange("p e j a -> p (j a) e"),
                 bank[7][:, :].rearrange("p (b e) -> p b e", e=E)).then_inc(vec_chain, 1)
            chain[0] += 1
            copy(b2_cols[:, :, :], bank[4][:, 0:KC * E].rearrange("p (f e) -> p f e", e=E)).then_inc(vec_bT, 1)
            dve.wait_ge(pe_ada, 1)
            link(tt(mod[:, 0:16], bank[5][:, 0:16], cols[:, 0:16], ALU.add))
            link(stt(scale1[:, :], mod[:, 8:16], 1.0, cols[:, ROW_G1:ROW_G1 + 8], ALU.add, ALU.mult))
            dve.wait_ge(pe_xT, 1)
            for f in range(KC):
                ins = ts(hT[:, f, :], pair(f // 2)[:, f % 2, :], scale1[:, f:f + 1], mod[:, f:f + 1], ALU.mult, ALU.add)
            ins.then_inc(vec_hT, 1)

            for i in range(12):
                dve.wait_ge(pe_pair, i + 1)
                src = pair(i % 4)
                for j in range(TAPS - 1, -1, -1):
                    shift = TAPS - 1 - j
                    steps = []
                    for a in range(2):
                        f = 2 * i + a
                        w = conv_cols[:, j, f:f + 1]
                        if shift == 0:
                            steps.append(ts(qkv[:, f, :], src[:, a, :], w, None, ALU.mult))
                        else:
                            steps.append(stt(qkv[:, f, shift:S], src[:, a, 0:S - shift], w, qkv[:, f, shift:S],
                                             ALU.mult, ALU.add))
                    if j:
                        link(*steps)
                    else:
                        steps[1].then_inc(vec_conv, 1)
            dve.wait_ge(pe_ba, 1)
            dve.wait_ge(early_in, 16 * 6)
            tt(heads_in[:, APLUS], bank[4][:, 0:32].rearrange("p (t n) -> p t n", t=T)[:, :, 8:16],
               small[:, 0:8].unsqueeze(1).to_broadcast([P, T, HEADS]), ALU.add).then_inc(vec_ba, 1)
            dve.wait_ge(vec_ba, 1)
            stt(heads_in[:, MAG], heads_in[:, APLUS], -1.0, heads_in[:, APLUS], ALU.mult, ALU.max).then_inc(vec_ba, 1)
            for i in range(2):
                dve.wait_ge(pe_pair, 12 + i + 1)
                copy(u_pool[:, 2 * i:2 * i + 2, :], pair(i)).then_inc(vec_pair, 1)
            dve.wait_ge(vec_pair, 2)
            src, held = u_pool, (pool_a, pool_b)
            for i in range(4):
                dst, w = held[i % 2], 2 ** i
                link(tt(dst[:, i:4, w:S], src[:, i:4, w:S], src[:, i:4, 0:S - w], ALU.add),
                     copy(dst[:, i:4, 0:w], src[:, i:4, 0:w]))
                src = dst
            counts = const_tile("count").rearrange("p (g n) -> p g n", g=4)
            dve.wait_ge(const_in, 16)
            for i, w in enumerate(WINDOWS):
                src = held[i % 2]
                link(tt(pool_b[:, i, 0:16], src[:, i, 0:16], counts[:, i, :], ALU.mult),
                     stt(pool_b[:, i, 16:S], src[:, i, 16:S], 1.0 / w, u_pool[:, i, 16:S], ALU.mult, ALU.subtract))
            tt(pool_b[:, :, 0:16], pool_b[:, :, 0:16], u_pool[:, :, 0:16], ALU.subtract).then_inc(vec_pooled, 1)

            dve.wait_ge(act_ba, 2)
            u, denom, z, z2, acc = (heads_in[:, what] for what in (EMAG, ONEP, LN1P, MAG, KDF))
            link(ts(denom, u, 2.0, None, ALU.add))
            link(recip(denom, denom), ts(heads_in[:, APLUS], heads_in[:, APLUS], 0.0, None, ALU.max))
            link(tt(z, u, denom, ALU.mult))
            link(tt(z2, z, z, ALU.mult))
            link(ts(acc, z2, 1.0 / 17, None, ALU.mult))
            for odd in range(15, 1, -2):
                link(stt(acc, acc, 1.0 / odd, z2, ALU.add, ALU.mult))
            link(stt(acc, acc, 1.0, z, ALU.add, ALU.mult))
            link(stt(heads_in[:, LN1P], acc, 2.0, heads_in[:, APLUS], ALU.mult, ALU.add))
            stt(heads_in[:, G], heads_in[:, LN1P], -1.0, small[:, 24:32].unsqueeze(1).to_broadcast([P, T, HEADS]),
                ALU.mult, ALU.mult).then_inc(vec_g, 1)
            dve.wait_ge(pe_g, 1)
            rates = bank[6][:, 0:16].rearrange("p (t h) -> p t h", t=T)
            copy(heads_in[:, GC], rates).then_inc(vec_g, 1)
            dve.wait_ge(pe_ypool, 1)
            for i in range(4):
                ins = ts(y_pool[:, i, :], pair(4 + i // 2)[:, i % 2, :], cols[:, ROW_POOL + i:ROW_POOL + i + 1], None,
                         ALU.mult)
            ins.then_inc(vec_ypool, 1)
            dve.wait_ge(pe_g, 2)
            dve.wait_ge(vec_g, 2)
            copy(heads_in[:, KDF], rates).then_inc(vec_g, 1)
            for i in range(8):
                dve.wait_ge(act_norm, i + 1)
                link(recip(sq[:, i, :], sq[:, i, :]))
                a = qkv[:, 2 * i:2 * i + 2, :].rearrange("p a s -> p (a s)")
                tt(a, a, sq[:, i, :], ALU.mult).then_inc(vec_norm, 1)
            for i in range(4):
                dve.wait_ge(pe_pair, 18 + i + 1)
                a = region_y[:, 2 * i:2 * i + 2, :]
                dve.wait_ge(act_pair, i + 1)
                tt(a, a, pair((18 + i) % 4), ALU.mult).then_inc(vec_pair, 1)
            dve.wait_ge(act_ba, 3)
            link(tt(heads_in[:, BEG], heads_in[:, BETA], heads_in[:, EG], ALU.mult))

            dve.wait_ge(vec_g, 3)
            dve.wait_ge(vec_norm, 8)
            for g in range(2):
                def head(what, t, h):
                    return heads_in[:, what, t, HG * g + h:HG * g + h + 1]

                def heads(what, t):
                    return per_head(heads_in[:, what, t, HG * g:HG * g + HG])

                for t in range(T):
                    for h in range(HG):
                        ins = ts(prod[:, t, h], ident, head(GC, t, h), None, ALU.mult)
                    ins.then_inc(vec_diag, 1)
                for t in range(T):
                    dve.wait_ge(pe_grow, 2 * g + t + 1)
                    for h in range(HG):
                        ts(decay[:, t, h], quad(3 * t)[:, h], head(GC, t, h), 0.0, ALU.subtract, ALU.max)
                    for h in range(HG):
                        ins = ts(decayT[:, t, h], quad(3 * t)[:, h], head(GC, t, h), 0.0, ALU.subtract, ALU.min)
                    ins.then_inc(vec_darg, 1)
                for t in range(T):
                    dve.wait_ge(pe_kk, 2 * g + t + 1)
                    dve.wait_ge(pool_decay, 2 * g + t + 1)
                    tt(decayT[:, t], quad(3 * t + 2), decayT[:, t], ALU.mult)
                    a = q_of[:, HG * g:HG * g + HG, t * P:(t + 1) * P]
                    tt(a, a, eg_row[:, t], ALU.mult)
                    for h in range(HG):
                        ins = stt(decay[:, t, h], quad(3 * t + 1)[:, h], head(BETA, t, h), decay[:, t, h],
                                  ALU.mult, ALU.mult)
                    ins.then_inc(vec_l, 1)
                for t in range(T):
                    dve.wait_ge(pe_nat, 2 * g + t + 1)
                    tt(vb[:, t], quad(3 * t + 2), heads(BETA, t), ALU.mult)
                    tt(kbg[:, t], quad(3 * t + 1), heads(BEG, t), ALU.mult)
                    tt(kdec[:, t], quad(3 * t + 1), heads(KDF, t), ALU.mult).then_inc(vec_nat, 1)
                    dve.wait_ge(pe_lT, 2 * g + t + 1)
                    copy(lT[:, t], quad(3 * t)).then_inc(vec_lT, 1)
                for t in range(T):
                    dve.wait_ge(pool_off, 14 * g + 2 * t + 1)
                    stt(inv[:, t], inv[:, t], -1.0, over_heads(ident), ALU.mult, ALU.add)
                    dve.wait_ge(pool_off, 14 * g + 2 * t + 2)
                    stt(invT[:, t], invT[:, t], -1.0, over_heads(ident), ALU.mult, ALU.add).then_inc(vec_inv, 1)
                for i in range(5):
                    for t in range(T):
                        dve.wait_ge(vec_inv, 12 * g + 2 * i + t + 1)
                        dve.wait_ge(pe_corr, 10 * g + 2 * i + t + 1)
                        if i < 4:
                            tt(inv[:, t], inv[:, t], quad(3 * t), ALU.subtract)
                        tt(invT[:, t], invT[:, t], quad(3 * t + 2), ALU.subtract).then_inc(vec_inv, 1)
                for t in range(T):
                    dve.wait_ge(act_u, 2 * g + t + 1)
                    copy(kbg[:, t], quad(3 * t + 1)).then_inc(vec_w, 1)
                dve.wait_ge(act_u, 2 * g + 2)
                for ci in range(S // CHUNK):
                    t, lo = ci // 2, CHUNK * (ci % 2)
                    rows_c = slice(lo, lo + CHUNK)
                    if ci:
                        dve.wait_ge(pe_ws, 3 * g + ci)
                        tt(vb[rows_c, t], vb[rows_c, t], quad(3 * t)[rows_c], ALU.subtract).then_inc(vec_vnew, 1)
                        dve.wait_ge(vec_state, 3 * g + ci)
                    dve.wait_ge(pe_o, 4 * g + ci + 1)
                    if ci == 0:
                        copy(state, quad(3 * t + 2)).then_inc(vec_state, 1)
                    elif ci < S // CHUNK - 1:
                        for h in range(HG):
                            ins = stt(state[:, h], state[:, h], eg_row[:, t, h, lo + CHUNK - 1:lo + CHUNK],
                                      quad(3 * t + 2)[:, h], ALU.mult, ALU.add)
                        ins.then_inc(vec_state, 1)
                    if ci % 2:
                        copy(o_nat[:, g, t], quad(3 * t + 1)).then_inc(vec_o, 1)
            dve.wait_ge(pe_ada2, 1)
            link(tt(mod[:, 16:48], bank[6][:, 0:32], cols[:, 16:48], ALU.add))
            dve.wait_ge(vec_bT, 1)
            stt(scale2[:, :], mod[:, 32:40], 1.0, cols[:, ROW_G2:ROW_G2 + 8], ALU.add, ALU.mult).then_inc(vec_mod2, 1)
            tt(b2_cols[:, :, :], b2_cols[:, :, :], mod[:, 40:48].unsqueeze(2).to_broadcast([P, KC, E]), ALU.mult)
            dve.wait_ge(pool_osq, 1)
            nc.vector.tensor_reduce(small[:, 32:48], o_sq.rearrange("p (a n) -> p a n", n=P), AX.X, ALU.add)\
                .then_inc(vec_ossq, 1)
            dve.wait_ge(act_orms, 1)
            link(recip(small[:, 32:48], small[:, 32:48]))
            a = v_of.rearrange("p h s -> p (h s)").rearrange("p (a n) -> p a n", n=P)
            tt(a, a, small[:, 32:48].unsqueeze(2).to_broadcast([P, 16, P]), ALU.mult).then_inc(vec_on, 1)
            dve.wait_ge(pe_oT, 1)
            dve.wait_ge(act_zs, 1)
            for i in range(4):
                a = region_z[:, 2 * i:2 * i + 2, :]
                stt(a, pair(i), cols[:, ROW_GDN:ROW_GDN + 1], a, ALU.mult, ALU.mult).then_inc(vec_yg, 1)
            for i in range(4):
                dve.wait_ge(pe_tail, 4 + i + 1)
                dve.wait_ge(act_gate1, i + 1)
                a, y = gate1[:, 2 * i:2 * i + 2, :], region_y[:, 2 * i:2 * i + 2, :]
                link(tt(a, a, pair(i), ALU.mult))
                tt(y, y, a, ALU.add).then_inc(vec_tail, 1)
            for i in range(4):
                dve.wait_ge(pe_tail, 8 + i + 1)
                for f in (2 * i, 2 * i + 1):
                    ins = ts(moT[:, f, :], pair(4 + i)[:, f % 2, :], mod[:, 16 + f:17 + f], None, ALU.mult)
                ins.then_inc(vec_tail, 1)
            dve.wait_ge(x_in, 16 * 2 * T)
            for t in range(T):
                for half in range(2):
                    dve.wait_ge(pe_mo, 2 * t + half + 1)
                    a = xt[:, t, half * 512:(half + 1) * 512]
                    tt(a, a, bank[2 * t + half][:, :], ALU.add).then_inc(vec_x1, 1)
            dve.wait_ge(vec_x1, 4)
            dve.wait_ge(act_x1sq, 3)
            link(recip(stat[:, 1, 2:4], stat[:, 1, 2:4]))
            for t in range(T):
                ts(xn2[:, t, :], xt[:, t, :], stat[:, 1, 2 + t:3 + t], None, ALU.mult).then_inc(vec_xn2, 1)
            dve.wait_ge(vec_mod2, 1)
            for f in range(KC):
                dve.wait_ge(pe_h2T, f // 2 + 1)
                ins = ts(h2T[:, f, :], pair(4 + f // 2)[:, f % 2, :], scale2[:, f:f + 1], mod[:, 24 + f:25 + f],
                         ALU.mult, ALU.add)
            ins.then_inc(vec_h2T, 1)

            dve.wait_ge(pe_logits, 1)
            link(tt(logits, bank[4][:, 0:2 * E].rearrange("p (t e) -> p t e", t=T),
                    rb[:, :].unsqueeze(1).to_broadcast([P, T, E]), ALU.add))
            link(*(nc.vector.max(top[:, t, :], logits[:, t, :]) for t in range(T)))
            link(*(nc.vector.max_index(top_i[:, t, :], top[:, t, :], logits[:, t, :]) for t in range(T)))
            link(copy(idx, top_i[:, :, :]))
            for t in range(T):
                ins = ts(expw[:, t, 0:4], top[:, t, 0:4], top[:, t, 0:1], None, ALU.subtract)
            ins.then_inc(vec_logits, 1)
            lanes = const_tile("iota")[:, 0:E]
            link(*(ts(mask[:, t, :], lanes, idx[:, t, 0:1], None, ALU.is_equal) for t in range(T)))
            for rk in range(1, TOPK):
                steps = [stt(mask[:, t, :], lanes, idx[:, t, rk:rk + 1], mask[:, t, :], ALU.is_equal, ALU.add)
                         for t in range(T)]
                if rk < TOPK - 1:
                    link(*steps)
                else:
                    steps[-1].then_inc(vec_mask, 1)
            dve.wait_ge(act_top, 1)
            link(nc.vector.tensor_reduce(expw[:, :, 4:5], expw[:, :, 0:4], AX.X, ALU.add))
            link(recip(expw[:, :, 4:5], expw[:, :, 4:5]))
            link(tt(expw[:, :, 0:4], expw[:, :, 0:4], expw[:, :, 4:5].to_broadcast([P, T, 4]), ALU.mult))
            link(*(ts(gatew[:, t, :], lanes, idx[:, t, 0:1], expw[:, t, 0:1], ALU.is_equal, ALU.mult) for t in range(T)))
            for rk in range(1, TOPK):
                link(*(ts(hot[:, t, :], lanes, idx[:, t, rk:rk + 1], expw[:, t, rk:rk + 1], ALU.is_equal, ALU.mult)
                       for t in range(T)))
                link(tt(gatew, gatew, hot, ALU.add))
            dve.wait_ge(pe_rank, 1)
            dve.wait_ge(vec_mask, 1)
            link(nc.vector.memset(slot_of[:, :, E:E + 1], -1.0),
                 stt(slot_of[:, :, 0:E], bank[5][:, 0:2 * E].rearrange("p (t e) -> p t e", t=T), 1.0, mask,
                     ALU.add, ALU.mult),
                 nc.vector.tensor_reduce(idx[:, 0, 0:1], bank[5][:, 2 * E:3 * E], AX.X, ALU.max))
            link(ts(slot_of[:, :, 0:E], slot_of[:, :, 0:E], -1.0, None, ALU.add),
                 ts(idx[:, 0, 1:2], idx[:, 0, 0:1], float(SLOTS), 1.0, ALU.is_gt, ALU.add))
            for k in range(2, ROUNDS):
                link(ts(idx[:, 1, 0:1], idx[:, 0, 0:1], float(SLOTS * k), None, ALU.is_gt))
                link(tt(idx[:, 0, 1:2], idx[:, 0, 1:2], idx[:, 1, 0:1], ALU.add))
            copy(rounds_i[:, :], idx[:, 0, 1:2]).then_inc(vec_route, 1)

            LINKS = 12
            ROUND_LINKS = E * LINKS + 1

            def moe(r):
                n0 = r * E

                def select(e):
                    for t in range(T):
                        ins = ts(sel[:, t, :], const_tile("iota"), slot_of[:, t, bass.ds(e, 1)], None, ALU.is_equal)
                    ins.then_inc(vec_sel, 1)

                def body(n, e, first_expert=False):
                    count = [0]

                    def link(ins):
                        count[0] += 1
                        ins.then_inc(moe_chain, 1)
                        dve.wait_ge(moe_chain, n * LINKS + r + 1 + count[0])

                    if not first_expert:
                        dve.wait_ge(pe_selT, n)
                    for t in range(T):
                        ts(wsel[:, t, :], const_tile("iota"), slot_of[:, t, bass.ds(e, 1)],
                           gatew[:, t, bass.ds(e, 1)], ALU.is_equal, ALU.mult)
                    select(e + 1)
                    for j in range(4):
                        dve.wait_ge(used[j], n + USES + 1)
                        if j or not first_expert or not isinstance(r, int):
                            dve.wait_ge(vec_act, 4 * n + j)
                        link(tt(hu[:, :, :], bank[j % 2][:, 0:4 * SLOTS].rearrange("p (b s) -> p b s", b=4),
                                b1_cols[:, bass.ds(e, 1), j, :].rearrange("p e a -> p (e a)").unsqueeze(2)
                                .to_broadcast([P, 4, SLOTS]), ALU.add))
                        ts(hu[:, :, :], hu[:, :, :], LIMIT, None, ALU.min).then_inc(vec_hu, 1)
                        dve.wait_ge(vec_hu, 4 * n + j + 1)
                        link(ts(hu[:, 2:4, :], hu[:, 2:4, :], -LIMIT, 1.0, ALU.max, ALU.add))
                        link(tt(hu[:, 2:4, :], hu[:, 2:4, :], hu[:, 0:2, :], ALU.mult))
                        dve.wait_ge(act_sig, 4 * n + j + 1)
                        tt(actT[:, 2 * j:2 * j + 2, :], hu[:, 2:4, :], sig[:, :, :], ALU.mult).then_inc(vec_act, 1)
                        if j == 0 and not first_expert:
                            y_rows(n)
                    assert count[0] == LINKS
                    x_cols(n + r + 2)

                def x_cols(count):
                    dve.wait_ge(pe_gather, count)
                    copy(xT[:, 0:4, :], bank[2][:, 0:4 * SLOTS].rearrange("p (b s) -> p b s", b=4)).then_inc(vec_xT, 1)

                def y_rows(n):
                    dve.wait_ge(pe_yn, n)
                    copy(y_nat[:, 0:512], bank[2][0:SLOTS, :]).then_inc(vec_yn, 1)

                if isinstance(r, int):
                    ts(slot_of[:, :, :], slot_of[:, :, :], 0.0, None, ALU.add).then_inc(moe_chain, 1)
                else:
                    dve.wait_ge(pe_selT, n0)
                    dve.wait_ge(vec_sel, n0 + r)
                    ts(slot_of[:, :, :], slot_of[:, :, :], -float(SLOTS), None, ALU.add).then_inc(moe_chain, 1)
                dve.wait_ge(moe_chain, n0 * LINKS + r + 1)
                select(0)
                x_cols(n0 + r + 1)
                body(n0, 0, first_expert=True)
                with dve.Fori(1, E) as e:
                    body(n0 + e, e)
                y_rows(n0 + E)

            rounds(dve, moe)
            dve.wait_ge(act_fin, 4)
            sums = stat[:, 0, :].rearrange("p (t a) -> p t a", t=T)
            tt(stat[:, 1, 0:2].unsqueeze(2), sums[:, :, 0:1], sums[:, :, 1:2], ALU.add).then_inc(vec_fin, 1)
            dve.wait_ge(act_fin, 5)
            recip(stat[:, 1, 2:4], stat[:, 1, 0:2]).then_inc(vec_fin, 1)
            dve.wait_ge(vec_fin, 2)
            dve.wait_ge(fin_in, 16)
            for t in range(T):
                for half in range(2):
                    cut_ = slice(half * 512, (half + 1) * 512)
                    ins = stt(fin[:, t, cut_], bank[4 + 2 * t + half][:, :], stat[:, 1, 2 + t:3 + t], fin_g[:, cut_],
                              ALU.mult, ALU.mult)
                ins.then_inc(vec_out, 1)


_INS = ["x", "c", "ada_w", "ada_b", "norm_mix_g", "norm_ffn_g", "w_in", "conv_w", "pool_w", "pool_scale", "a_log",
        "dt_bias", "gdn_norm_g", "w_pool_out", "w_gdn_out", "w_out", "router_w", "router_b", "exp_w1", "exp_b1",
        "exp_w2", "exp_b2", "final_norm_g"]
_OUT = (1, S, D)


def kernel(**inputs):
    import numpy as _np
    import concourse.bacc as _bacc
    from concourse import mybir as _mybir
    from concourse.bass_utils import run_bass_kernel_spmd as _run

    nc = _bacc.Bacc("TRN2", target_bir_lowering=False, num_devices=1)
    arrays, args = {}, []
    for name in _INS:
        a = _np.ascontiguousarray(inputs[name])
        arrays[f"in_{name}_dram"] = a
        args.append(nc.dram_tensor(f"in_{name}_dram", a.shape, _mybir.dt.from_np(a.dtype), kind="ExternalInput").ap())
    arrays["in_const_dram"] = constants()
    args.append(nc.dram_tensor("in_const_dram", (P, CONST_W), _mybir.dt.float32, kind="ExternalInput").ap())
    args.append(nc.dram_tensor("out_0_dram", _OUT, _mybir.dt.float32, kind="ExternalOutput").ap())
    program(nc, *args)
    r = _run(nc, [arrays], core_ids=[0])
    return r.results[0]["out_0_dram"]
```

```python
from contextlib import ExitStack

import numpy as np
import concourse.bass as bass
from concourse import mybir

F32 = mybir.dt.float32
I32 = mybir.dt.int32
U32 = mybir.dt.uint32
ALU = mybir.AluOpType
ACT = mybir.ActivationFunctionType
AX = mybir.AxisListType

P = 128
D = 1024
S = 256
T = S // P
KC = D // P
HEADS = 8
HG = 4
CHUNK = 64
WINDOWS = (2, 4, 8, 16)
POOL_W = 512
GDN_W = 1024
TAPS = 4
E = 32
TOPK = 4
SLOTS = 64
HALF = 256
MAX_BLOCKS = E + TOPK * S // SLOTS
RING = 6
CW = 512
EPS = 1e-6
LIMIT = 7.0
ALPHA = 1.702

COL_POOL = 0
COL_QKV = POOL_W
COL_Z = COL_QKV + 3 * GDN_W
COL_BA = COL_Z + GDN_W
COL_GATE = COL_BA + 2 * HEADS

ROW_ADA_B = 0
ROW_C = 48
ROW_G1 = 56
ROW_G2 = 64
ROW_POOL = 72
ROW_GDN = 76
ROWS = 77

CONST = {}
_at = 0
for _name, _w in (("ident", P), ("ones", P), ("causal", P), ("after", P), ("strict", P), ("before", P),
                  ("off1", P), ("off1T", P), ("off2T", P), ("off4T", P), ("off8T", P), ("off16T", P),
                  ("off32T", P), ("iota", S), ("row", 1),
                  ("pick", 2 * 2 * HEADS - 1), ("qscale", 1), ("count", len(WINDOWS) * 16)):
    CONST[_name] = (_at, _w)
    _at += _w
CONST_W = _at


def constants():
    c = np.zeros((P, CONST_W), np.float32)
    r, q = np.meshgrid(np.arange(P), np.arange(P), indexing="ij")
    same = r // CHUNK == q // CHUNK

    def put(name, a):
        o, w = CONST[name]
        c[:, o:o + w] = a

    put("ident", r == q)
    put("ones", 1.0)
    put("causal", same & (r <= q))
    put("after", same & (r > q))
    put("strict", same & (r > q))
    put("before", r < q)
    for s in (1, 2, 4, 8, 16, 32):
        off = (r // (2 * s) == q // (2 * s)) & (q // s % 2 == 1) & (r // s % 2 == 0)
        put(f"off{s}T", off)
        if s == 1:
            put("off1", off.T)
    put("iota", np.arange(S))
    put("row", np.arange(P)[:, None])
    put("pick", np.arange(2 * 2 * HEADS - 1) == 2 * HEADS - 1)
    put("qscale", np.where(np.arange(P) < HEADS, P, 1)[:, None])
    t = np.arange(16)
    put("count", np.concatenate([1.0 / np.minimum(t + 1, w) for w in WINDOWS]))
    return c


def program(nc, x, c, ada_w, ada_b, norm_mix_g, norm_ffn_g, w_in, conv_w, pool_w, pool_scale, a_log,
            dt_bias, gdn_norm_g, w_pool_out, w_gdn_out, w_out, router_w, router_b, exp_w1, exp_b1,
            exp_w2, exp_b2, final_norm_g, const, out):
    with ExitStack() as ctx:
        ctx.enter_context(nc.allow_non_contiguous_dma(reason="small parameter rows"))

        def sb(name, shape, dt=F32):
            return ctx.enter_context(nc.sbuf_tensor(name, shape, dt))

        def sem(name):
            return ctx.enter_context(nc.semaphore(name))

        ring = sb("ring", [P, RING, KC, CW])
        consts = sb("consts", [P, CONST_W])
        region_x = sb("region_x", [P, 2048])
        region_h = sb("region_h", [P, 2048])
        qkv = sb("qkv", [P, 24, S])
        region_y = sb("region_y", [P, KC, S])
        region_z = sb("region_z", [P, HEADS, S])
        work = sb("work", [P, 9728])
        cols = sb("cols", [P, ROWS])
        conv_cols = sb("conv_cols", [P, TAPS, 24])
        mod = sb("mod", [P, 48])
        scale1 = sb("scale1", [P, KC])
        scale2 = sb("scale2", [P, KC])
        c_act = sb("c_act", [P, KC])
        rw = sb("rw", [P, KC, E])
        rb = sb("rb", [P, E])
        stat = sb("stat", [P, 2, 4])
        heads_in = sb("heads_in", [P, 11, T, HEADS])
        top = sb("top", [P, T, 8])
        top_i = sb("top_i", [P, T, 8], U32)
        small = sb("small", [P, 48])
        blocks_i = sb("blocks_i", [1, 2 * P + 1], I32)

        def const_tile(name):
            o, w = CONST[name]
            return consts[:, o:o + w]

        ident = const_tile("ident")
        ones = const_tile("ones")

        def over_heads(tile):
            return tile.unsqueeze(1).to_broadcast([P, HG, P])

        def per_head(a):
            return a.unsqueeze(2).to_broadcast([P, HG, P])

        xt = region_x[:, :].rearrange("p (t d) -> p t d", t=T)
        hT = region_h[:, :].rearrange("p (c s) -> p c s", c=KC)
        q_of, k_of, v_of = (qkv[:, i * HEADS:(i + 1) * HEADS, :] for i in range(3))
        BETA, APLUS, MAG, EMAG, ONEP, LN1P, G, GC, EG, KDF, BEG = range(11)

        sq = work[:, 0:4096].rearrange("p (i n) -> p i n", i=8)
        norms = work[0:2 * HEADS, 0:S]
        u_pool = work[:, 4096:5120].rearrange("p (g s) -> p g s", g=4)
        pool_a = work[:, 5120:6144].rearrange("p (g s) -> p g s", g=4)
        pool_b = work[:, 6144:7168].rearrange("p (g s) -> p g s", g=4)
        y_pool = work[:, 7168:8192].rearrange("p (g s) -> p g s", g=4)
        pw = work[:, 8192:8704].rearrange("p (g n) -> p g n", g=4)
        wba = work[:, 8704:8832].rearrange("p (c n) -> p c n", c=KC)
        rows = work[:, 8832:8960]
        conv_rows = work[:, 8960:9088]
        ada_sum = region_z[:, :, :].rearrange("p (b a h) s -> p b a (h s)", b=2, a=2)

        def matrices(tensor, i):
            return tensor[:, i * 1024:(i + 1) * 1024].rearrange("p (t h n) -> p t h n", t=T, h=HG)

        decay = matrices(region_x, 0)
        decayT = matrices(region_x, 1)
        lT, inv, invT, prod, off, eg_row, vb, kbg, kdec = (matrices(work, i) for i in range(9))
        state = work[:, 9216:9728].rearrange("p (h n) -> p h n", h=HG)
        o_nat = qkv[:, 16:24, :].rearrange("p (g a) s -> p g (a s)", g=2) \
            .rearrange("p g (t h n) -> p g t h n", t=T, h=HG)
        o_flat = qkv[:, 16:24, :].rearrange("p (b a) s -> p b (a s)", b=4)
        o_sq = work[:, 0:2048].rearrange("p (b n) -> p b n", b=4)

        gate1 = k_of
        moT = q_of
        xn2 = k_of.rearrange("p h s -> p (h s)").rearrange("p (t d) -> p t d", t=T)
        h2T = hT
        h2 = v_of.rearrange("p h s -> p (h s)").rearrange("p (t d) -> p t d", t=T)

        m = 0

        def take(n, parts=P):
            nonlocal m
            a = work[0:parts, m:m + n]
            m += n
            return a

        b8 = region_y[:, :, :].rearrange("p c s -> p (c s)")
        sel = take(T * SLOTS).rearrange("p (t s) -> p t s", t=T)
        wsel = take(T * SLOTS).rearrange("p (t s) -> p t s", t=T)
        wselT = take(T * P, SLOTS)
        xT = take(KC * SLOTS).rearrange("p (c s) -> p c s", c=KC)
        actT = take(KC * SLOTS).rearrange("p (c s) -> p c s", c=KC)
        hu = take(2 * P).rearrange("p (b s) -> p b s", b=2)
        sig = take(P)
        act_nat = take(2 * P).rearrange("p (b s) -> p b s", b=2)
        onehot = take(SLOTS)
        fin = take(T * D).rearrange("p (t d) -> p t d", t=T)
        y_nat = take(D, SLOTS)
        fin_g = take(D)
        b1_rows = take(2 * D)
        b2_rows = take(D, E)
        z_flat = region_z[:, :, :].rearrange("p h s -> p (h s)")
        gt2_row = z_flat[:, 0:D]
        gt2_diag = z_flat[:, D:2 * D].rearrange("p (f n) -> p f n", f=KC)
        gatewT = b8[0:E, 512:768]
        blocks_row = b8[0:E, 768:896]
        upto = b8[:, 896:928]
        ends = b8[:, 928:960]
        block_cols = b8[:, 960:964]
        counts_e = b8[0:E, 964:966]
        logits = b8[:, 0:64].rearrange("p (t e) -> p t e", t=T)
        idx = b8[:, 96:112].rearrange("p (t n) -> p t n", t=T)
        hot = b8[:, 128:192].rearrange("p (t e) -> p t e", t=T)
        mask = b8[:, 192:256].rearrange("p (t e) -> p t e", t=T)
        gatew = b8[:, 256:320].rearrange("p (t e) -> p t e", t=T)
        slot_of = b8[:, 320:384].rearrange("p (t e) -> p t e", t=T)
        expw = b8[:, 452:468].rearrange("p (t n) -> p t n", t=T)

        bank = [ctx.enter_context(nc.psum_tensor(f"bank{i}", [P, 512], F32)) for i in range(8)]

        def pair(i):
            return bank[i][:, :].rearrange("p (a s) -> p a s", a=2)

        def quad(i):
            return bank[i][:, :].rearrange("p (h n) -> p h n", h=HG)

        const_in = sem("const_in")
        rows_in = sem("rows_in")
        x_in = sem("x_in")
        early_in = sem("early_in")
        b_in = sem("b_in")
        fin_in = sem("fin_in")
        out_done = sem("out_done")
        landed = [sem(f"landed{i}") for i in range(RING)]
        used = [sem(f"used{i}") for i in range(RING)]

        vec_chain = sem("vec_chain")
        pool_chain = sem("pool_chain")

        pe_rows = sem("pe_rows")
        vec_cols = sem("vec_cols")
        act_c = sem("act_c")
        act_xsq = sem("act_xsq")
        act_xrms = sem("act_xrms")
        vec_xn = sem("vec_xn")
        pe_xT = sem("pe_xT")
        vec_adastep = sem("vec_adastep")
        vec_ada = sem("vec_ada")
        pe_ada = sem("pe_ada")
        vec_hT = sem("vec_hT")
        pe_pair = sem("pe_pair")
        vec_pair = sem("vec_pair")
        act_pair = sem("act_pair")
        vec_conv = sem("vec_conv")
        act_silu = sem("act_silu")
        pe_ba = sem("pe_ba")
        vec_ba = sem("vec_ba")
        act_ba = sem("act_ba")
        vec_pooled = sem("vec_pooled")
        pe_ypool = sem("pe_ypool")
        vec_ypool = sem("vec_ypool")
        pool_sq = sem("pool_sq")
        pe_ssq = sem("pe_ssq")
        act_norm = sem("act_norm")
        vec_rnorm = sem("vec_rnorm")
        pe_norm = sem("pe_norm")
        vec_norm = sem("vec_norm")
        vec_g = sem("vec_g")
        pe_g = sem("pe_g")

        vec_diag = sem("vec_diag")
        pe_grow = sem("pe_grow")
        pe_kk = sem("pe_kk")
        vec_darg = sem("vec_darg")
        act_decay = sem("act_decay")
        pool_decay = sem("pool_decay")
        vec_l = sem("vec_l")
        pe_nat = sem("pe_nat")
        vec_nat = sem("vec_nat")
        pe_lT = sem("pe_lT")
        vec_lT = sem("vec_lT")
        pool_off = sem("pool_off")
        vec_inv = sem("vec_inv")
        pe_prod = sem("pe_prod")
        act_prod = sem("act_prod")
        pe_corr = sem("pe_corr")
        pe_uw = sem("pe_uw")
        act_u = sem("act_u")
        vec_w = sem("vec_w")
        pe_ws = sem("pe_ws")
        vec_vnew = sem("vec_vnew")
        pe_o = sem("pe_o")
        vec_state = sem("vec_state")
        vec_o = sem("vec_o")
        pe_z = sem("pe_z")
        act_z = sem("act_z")
        pool_osq = sem("pool_osq")
        vec_ossq = sem("vec_ossq")
        act_orms = sem("act_orms")
        vec_on = sem("vec_on")
        pe_oT = sem("pe_oT")
        vec_yg = sem("vec_yg")
        vec_mod2 = sem("vec_mod2")
        pe_tail = sem("pe_tail")
        pe_gate1 = sem("pe_gate1")
        act_gate1 = sem("act_gate1")
        vec_tail = sem("vec_tail")
        pe_mo = sem("pe_mo")
        vec_x1 = sem("vec_x1")
        act_x1sq = sem("act_x1sq")
        vec_xn2 = sem("vec_xn2")
        pe_h2T = sem("pe_h2T")
        vec_h2T = sem("vec_h2T")
        pe_h2 = sem("pe_h2")
        act_h2 = sem("act_h2")
        pe_logits = sem("pe_logits")
        vec_logits = sem("vec_logits")
        act_top = sem("act_top")
        vec_mask = sem("vec_mask")
        pe_rank = sem("pe_rank")
        vec_route = sem("vec_route")

        vec_sel = sem("vec_sel")
        pe_gather = sem("pe_gather")
        act_xT = sem("act_xT")
        vec_hu = sem("vec_hu")
        act_sig = sem("act_sig")
        vec_act = sem("vec_act")
        pe_selT = sem("pe_selT")
        act_selT = sem("act_selT")
        moe_chain = sem("moe_chain")
        pe_moe = sem("pe_moe")
        vec_wsel = sem("vec_wsel")
        vec_onehot = sem("vec_onehot")
        pe_actT = sem("pe_actT")
        act_actT = sem("act_actT")
        vec_y = sem("vec_y")
        vec_gatew = sem("vec_gatew")
        pe_gatewT = sem("pe_gatewT")
        vec_diag2 = sem("vec_diag2")
        pe_gt2 = sem("pe_gt2")
        vec_b2 = sem("vec_b2")
        vec_counts = sem("vec_counts")
        pe_ends = sem("pe_ends")
        vec_blocks = sem("vec_blocks")
        pe_blocks = sem("pe_blocks")
        act_fin = sem("act_fin")
        vec_fin = sem("vec_fin")
        vec_out = sem("vec_out")

        def cut(w, lo, n=CW):
            return w[0, :, lo:lo + n].rearrange("(c p) n -> p c n", p=P)

        def slot_as(i, c):
            return ring[:, i, :, :].rearrange("p c n -> p (c n)").rearrange("p (c n) -> p c n", c=c)

        chunks = [("ada", cut(ada_w, CW * i)) for i in range(4)]
        for i in range(6):
            chunks += [("qkv", cut(w_in, COL_QKV + CW * i)), ("ada2", cut(ada_w, CW * (4 + i)))]
        chunks += [("ada2", cut(ada_w, CW * 10)), ("pool", cut(w_in, COL_POOL)), ("ada2", cut(ada_w, CW * 11))]
        chunks += [("gate0", cut(w_in, COL_GATE + CW * i)) for i in range(2)]
        chunks += [("pool_out", w_pool_out[0].rearrange("(c p) n -> p c n", p=P))]
        chunks += [("z", cut(w_in, COL_Z + CW * i)) for i in range(2)]
        chunks += [("gate1", cut(w_in, COL_GATE + D + CW * i)) for i in range(2)]
        chunks += [("gdn_out", cut(w_gdn_out, CW * i)) for i in range(2)]
        chunks += [("w_out", cut(w_out, CW * i)) for i in range(2)]
        chunk_no = {}
        for n, (kind, _) in enumerate(chunks):
            chunk_no.setdefault(kind, []).append(n)
        USES = len(chunks) // RING
        assert len(chunks) % RING == 0

        w1_dram = exp_w1.rearrange("l e (c p) n -> (l e) p c n", p=P)
        w2_dram = exp_w2.rearrange("l e (c p) n -> (l e) p c n", p=P)

        def w_slot(n, j, k):
            return ring[:, n % RING, k, j * P:(j + 1) * P]

        block = ctx.enter_context(nc.Block())

        def further_blocks(eng, body):
            eng.wait_ge(vec_route, 1)
            count = eng.value_load(blocks_i[0:1, 2 * P:2 * P + 1], min_val=E, max_val=MAX_BLOCKS)
            with eng.Fori(1, count) as n:
                body(n)

        def at_least(eng, sem_, value):
            if not isinstance(value, int) or value > 0:
                eng.wait_ge(sem_, value)

        def expert_of(eng, n):
            return eng.value_load(blocks_i[0:1, bass.ds(n, 1)], min_val=0, max_val=E - 1)

        def start_of(eng, n):
            return eng.value_load(blocks_i[0:1, bass.ds(n + P, 1)], min_val=0, max_val=S - SLOTS)

        @block.sync
        def _(sp):
            sp.dma_start(rows[ROW_C:ROW_C + 8, :], c.rearrange("b (r n) -> (b r) n", n=P)).then_inc(rows_in, 16)
            sp.dma_start(rows[ROW_ADA_B:ROW_ADA_B + 48, :],
                         ada_b.rearrange("l (r n) -> (l r) n", n=P)).then_inc(rows_in, 16)
            sp.dma_start(consts[:, :], const).then_inc(const_in, 16)
            for t in range(T):
                sp.dma_start(xt[:, t, :], x[0, t * P:(t + 1) * P, :]).then_inc(x_in, 16)
            sp.wait_ge(rows_in, 16 * 10)
            for n, (kind, src) in enumerate(chunks):
                if n >= RING:
                    sp.wait_ge(used[n % RING], n // RING)
                dst = slot_as(n % RING, 4) if kind == "pool_out" else ring[:, n % RING, :, :]
                sp.dma_start(dst, src).then_inc(landed[n % RING], 16)

            def stream(n):
                e = 0 if isinstance(n, int) else expert_of(sp, n)
                for s in range(RING):
                    src = w1_dram[e, :, :, s * CW:(s + 1) * CW] if s < 4 else \
                        w2_dram[e, :, :, (s - 4) * CW:(s - 3) * CW]
                    sp.wait_ge(used[s], n + USES)
                    sp.dma_start(ring[:, s, :, :], src).then_inc(landed[s], 16)

            stream(0)
            further_blocks(sp, stream)
            for t in range(T):
                sp.wait_ge(vec_out, t + 1)
                sp.dma_start(out[0, t * P:(t + 1) * P, :], fin[:, t, :]).then_inc(out_done, 16)
            sp.wait_ge(out_done, 16 * T)

        @block.gpsimd
        def _(pool):
            chain = [0]

            def link(ins):
                chain[0] += 1
                ins.then_inc(pool_chain, 1)
                pool.wait_ge(pool_chain, chain[0])

            pool.dma_start(pw, pool_w[0].rearrange("g p n -> p g n")).then_inc(early_in, 16)
            pool.dma_start(wba, cut(w_in, COL_BA, 2 * HEADS)).then_inc(early_in, 16)
            pool.dma_start(small[:, 0:8], dt_bias[0].partition_broadcast(P)).then_inc(early_in, 16)
            pool.dma_start(small[:, 8:16], a_log[0].partition_broadcast(P)).then_inc(early_in, 16)
            pool.dma_start(rb[:, :], router_b[0].partition_broadcast(P)).then_inc(early_in, 16)
            pool.dma_start(rw[:, :, :], router_w[0].rearrange("(c p) n -> p c n", p=P)).then_inc(early_in, 16)

            for i in range(8):
                pool.wait_ge(act_silu, i + 1)
                src = qkv[:, 2 * i:2 * i + 2, :].rearrange("p a s -> p (a s)")
                nc.gpsimd.tensor_tensor(sq[:, i, :], src, src, ALU.mult).then_inc(pool_sq, 1)

            for g in range(2):
                for t in range(T):
                    b = 2 * g + t
                    pool.wait_ge(act_decay, b + 1)
                    nc.gpsimd.tensor_tensor(decay[:, t], decay[:, t], over_heads(const_tile("strict")), ALU.mult)
                    nc.gpsimd.tensor_tensor(decayT[:, t], decayT[:, t], over_heads(const_tile("causal")),
                                            ALU.mult).then_inc(pool_decay, 1)
                for t in range(T):
                    b = 2 * g + t
                    pool.wait_ge(vec_l, b + 1)
                    nc.gpsimd.tensor_tensor(inv[:, t], decay[:, t], over_heads(const_tile("off1")),
                                            ALU.mult).then_inc(pool_off, 1)
                    pool.wait_ge(vec_lT, b + 1)
                    nc.gpsimd.tensor_tensor(invT[:, t], lT[:, t], over_heads(const_tile("off1T")),
                                            ALU.mult).then_inc(pool_off, 1)
                for i, s in enumerate((2, 4, 8, 16, 32)):
                    for t in range(T):
                        if i:
                            pool.wait_ge(pe_prod, 10 * g + 2 * (i - 1) + t + 1)
                        nc.gpsimd.tensor_tensor(off[:, t], lT[:, t], over_heads(const_tile(f"off{s}T")),
                                                ALU.mult).then_inc(pool_off, 1)
            pool.wait_ge(vec_w, 4)
            for b in range(4):
                pool.wait_ge(vec_o, b + 1)
                nc.gpsimd.tensor_tensor(o_sq[:, b, :], o_flat[:, b, :], o_flat[:, b, :], ALU.mult).then_inc(pool_osq, 1)
            pool.wait_ge(vec_state, 6)
            link(nc.gpsimd.memset(b1_rows[:, :], 0.0))
            pool.dma_start(b1_rows[0:E, :], exp_b1[0]).then_inc(b_in, 16)
            pool.dma_start(b2_rows[:, :], exp_b2[0]).then_inc(b_in, 16)
            pool.dma_start(fin_g, final_norm_g.partition_broadcast(P)).then_inc(fin_in, 16)

        @block.scalar
        def _(act):
            for j in range(TAPS):
                act.dma_start(conv_rows[24 * j:24 * j + 24, :],
                              conv_w[0, j, :].rearrange("(r n) -> r n", n=P)).then_inc(rows_in, 16)
            for row, src, n in ((ROW_G1, norm_mix_g, 8), (ROW_G2, norm_ffn_g, 8), (ROW_POOL, pool_scale, 4),
                                (ROW_GDN, gdn_norm_g, 1)):
                act.dma_start(rows[row:row + n, :], src.rearrange("l (r n) -> (l r) n", n=P)).then_inc(rows_in, 16)

            act.wait_ge(vec_cols, 1)
            nc.scalar.activation(c_act[:, :], cols[:, ROW_C:ROW_C + 8], ACT.Silu).then_inc(act_c, 1)
            act.wait_ge(x_in, 16 * T)
            for t in range(T):
                nc.scalar.activation(region_y[:, 4 * t:4 * t + 4, :].rearrange("p c s -> p (c s)"), xt[:, t, :],
                                     ACT.Square, accum_out=stat[:, 0, t:t + 1]).then_inc(act_xsq, 1)
            act.wait_ge(act_xsq, 2)
            act.wait_ge(vec_cols, 2)
            nc.scalar.activation(stat[:, 0, 2:4], stat[:, 0, 0:2], ACT.Sqrt, scale=1.0 / D,
                                 bias=small[:, 16:17]).then_inc(act_xrms, 1)
            for i in range(12):
                act.wait_ge(vec_conv, i + 1)
                a = qkv[:, 2 * i:2 * i + 2, :]
                nc.scalar.activation(a, a, ACT.Silu).then_inc(act_silu, 1)
            act.wait_ge(pe_ba, 1)
            act.wait_ge(vec_ba, 1)
            nc.scalar.activation(heads_in[:, BETA], bank[4][:, 0:32].rearrange("p (t n) -> p t n", t=T)[:, :, 0:8],
                                 ACT.Sigmoid).then_inc(act_ba, 1)
            for i in range(4):
                if i == 2:
                    act.wait_ge(vec_ba, 2)
                    nc.scalar.activation(heads_in[:, EMAG], heads_in[:, MAG], ACT.Exp, scale=-1.0)
                    nc.scalar.activation(small[:, 24:32], small[:, 8:16], ACT.Exp).then_inc(act_ba, 1)
                act.wait_ge(pe_pair, 14 + i + 1)
                nc.scalar.activation(region_y[:, 2 * i:2 * i + 2, :], pair((14 + i) % 4),
                                     ACT.Sigmoid).then_inc(act_pair, 1)
            act.wait_ge(pe_ssq, 1)
            nc.scalar.activation(norms, bank[4][0:2 * HEADS, 0:S], ACT.Sqrt, scale=const_tile("qscale")[0:2 * HEADS, :],
                                 bias=small[0:2 * HEADS, 17:18]).then_inc(act_norm, 1)
            act.wait_ge(vec_g, 3)
            nc.scalar.activation(heads_in[:, EG], heads_in[:, GC], ACT.Exp)
            nc.scalar.activation(heads_in[:, KDF], heads_in[:, KDF], ACT.Exp).then_inc(act_ba, 1)

            def z_copy(i):
                act.wait_ge(pe_z, i + 1)
                nc.scalar.activation(region_z[:, 2 * i:2 * i + 2, :], pair(7), ACT.Silu).then_inc(act_z, 1)

            for g in range(2):
                for t in range(T):
                    b = 2 * g + t
                    act.wait_ge(vec_darg, b + 1)
                    nc.scalar.activation(eg_row[:, t], quad(3 * t), ACT.Exp)
                    nc.scalar.activation(decay[:, t], decay[:, t], ACT.Exp, scale=-1.0)
                    nc.scalar.activation(decayT[:, t], decayT[:, t], ACT.Exp).then_inc(act_decay, 1)
                z_copy(2 * g)
                z_copy(2 * g + 1)
                for i in range(5):
                    for t in range(T):
                        act.wait_ge(pe_prod, 10 * g + 2 * i + t + 1)
                        nc.scalar.activation(prod[:, t], quad(3 * t + 1), ACT.Copy).then_inc(act_prod, 1)
                for t in range(T):
                    act.wait_ge(pe_uw, 2 * g + t + 1)
                    nc.scalar.activation(vb[:, t], quad(3 * t), ACT.Copy).then_inc(act_u, 1)
            for i in range(4):
                act.wait_ge(pe_gate1, i + 1)
                nc.scalar.activation(gate1[:, 2 * i:2 * i + 2, :], pair(6 + i % 2), ACT.Sigmoid).then_inc(act_gate1, 1)
                for b in ((0, 1), (), (2,), (3,))[i]:
                    act.wait_ge(vec_ossq, b + 1)
                    a = small[:, 32 + HG * b:32 + HG * (b + 1)]
                    nc.scalar.activation(a, a, ACT.Sqrt, scale=1.0 / P, bias=small[:, 16:17]).then_inc(act_orms, 1)
            act.wait_ge(pe_o, 8)
            for t in range(T):
                act.dma_start(xt[:, t, :], x[0, t * P:(t + 1) * P, :]).then_inc(x_in, 16)
            act.wait_ge(vec_x1, 4)
            for t in range(T):
                nc.scalar.activation(moT[:, 4 * t:4 * t + 4, :].rearrange("p h s -> p (h s)"), xt[:, t, :],
                                     ACT.Square, accum_out=stat[:, 1, t:t + 1]).then_inc(act_x1sq, 1)
            act.wait_ge(act_x1sq, 2)
            nc.scalar.activation(stat[:, 1, 2:4], stat[:, 1, 0:2], ACT.Sqrt, scale=1.0 / D,
                                 bias=small[:, 16:17]).then_inc(act_x1sq, 1)
            for i in range(4):
                act.wait_ge(pe_h2, i + 1)
                nc.scalar.activation(h2[:, i // 2, (i % 2) * 512:(i % 2 + 1) * 512], bank[i][:, :],
                                     ACT.Copy).then_inc(act_h2, 1)
            act.wait_ge(vec_logits, 1)
            nc.scalar.activation(expw[:, :, 0:4], expw[:, :, 0:4], ACT.Exp).then_inc(act_top, 1)

            def gathered(count):
                act.wait_ge(pe_gather, count)
                nc.scalar.activation(xT.rearrange("p c s -> p (c s)"), bank[2][:, :], ACT.Copy).then_inc(act_xT, 1)

            def serve(n):
                for j in range(4):
                    act.wait_ge(vec_hu, 8 * n + 2 * j + 1)
                    nc.scalar.activation(sig, hu[:, 0, :], ACT.Sigmoid, scale=ALPHA).then_inc(act_sig, 1)
                    if j:
                        act.wait_ge(pe_actT, 4 * n + j)
                        nc.scalar.activation(actT[:, 2 * j - 2:2 * j, :].rearrange("p c s -> p (c s)"),
                                             bank[3][:, 256:384], ACT.Copy).then_inc(act_actT, 1)
                gathered(n + 2)
                act.wait_ge(pe_selT, n + 1)
                nc.scalar.activation(wselT, bank[3][0:SLOTS, 0:T * P], ACT.Copy).then_inc(act_selT, 1)
                act.wait_ge(pe_actT, 4 * n + 4)
                nc.scalar.activation(actT[:, 6:8, :].rearrange("p c s -> p (c s)"),
                                     bank[3][:, 256:384], ACT.Copy).then_inc(act_actT, 1)

            gathered(1)
            serve(0)
            further_blocks(act, serve)
            act.wait_ge(pe_moe, 1)
            for i in range(4):
                nc.scalar.activation(fin[:, i // 2, (i % 2) * 512:(i % 2 + 1) * 512], bank[4 + i][:, :], ACT.Square,
                                     accum_out=stat[:, 0, i:i + 1]).then_inc(act_fin, 1)
            act.wait_ge(vec_fin, 1)
            nc.scalar.activation(stat[:, 1, 0:2], stat[:, 1, 0:2], ACT.Sqrt, scale=1.0 / D,
                                 bias=small[:, 16:17]).then_inc(act_fin, 1)

        @block.tensor
        def _(pe):
            def arrived(n):
                pe.wait_ge(landed[n % RING], 16 * (n // RING + 1))

            done_chunk = []

            def free_slot(n):
                done_chunk.append(n)

            def carry(mm):
                if done_chunk:
                    mm.then_inc(used[done_chunk.pop() % RING], 1)

            def project(out_ap, n, j, rhs, kc=KC, w=None):
                for k in range(kc):
                    mm = nc.tensor.matmul(out_ap, w(k) if w else w_slot(n, j, k), rhs[:, k, :],
                                          start=(k == 0), stop=(k == kc - 1))
                    if k == 0:
                        carry(mm)
                return mm

            pe.wait_ge(const_in, 16)
            pe.wait_ge(rows_in, 16 * 10)
            nc.tensor.transpose(bank[6][:, 0:ROWS], rows[0:ROWS, :], ident[0:ROWS, 0:ROWS])
            nc.tensor.transpose(bank[6][:, 128:128 + 96], conv_rows[0:96, :], ident[0:96, 0:96]).then_inc(pe_rows, 1)
            pe.wait_ge(vec_xn, 2)
            for f in range(KC):
                for t in range(T):
                    mm = nc.tensor.transpose(pair(f // 2)[:, f % 2, t * P:(t + 1) * P],
                                             xt[:, t, f * P:(f + 1) * P], ident)
            mm.then_inc(pe_xT, 1)
            def ada_columns(n, out_ap):
                pe.wait_ge(vec_ada, n + 1)
                slot = (chunk_no["ada"] + chunk_no["ada2"])[n] % RING
                for j in range(4):
                    mm = nc.tensor.matmul(out_ap[:, j:j + 1], ada_sum[:, n % 2, 0, j * P:(j + 1) * P],
                                          ones[:, 0:1], start=True, stop=True)
                    if j == 0:
                        mm.then_inc(used[slot], 1)
                mm.then_inc(pe_ada, 1)

            for n in range(4):
                ada_columns(n, bank[5][:, 4 * n:4 * n + 4])
            pe.wait_ge(vec_hT, 1)
            released = {}
            for i in range(12):
                released[i] = (vec_conv, i + 1)
            for i in range(2):
                released[12 + i] = (vec_pair, i + 1)
            for i in range(4):
                released[14 + i] = (act_pair, i + 1)

            def pair_of(i, n, j, rhs, kc=KC, w=None):
                if i >= 4:
                    pe.wait_ge(*released[i - 4])
                for a in range(2):
                    mm = project(pair(i % 4)[:, a, :], n, j + a, rhs, kc, w and (lambda k, a=a: w(k, a)))
                mm.then_inc(pe_pair, 1)
                return mm

            def ada2_columns(m):
                ada_columns(4 + m, bank[7][:, 4 * m:4 * m + 4])

            for i in range(12):
                n = chunk_no["qkv"][i // 2]
                arrived(n)
                pair_of(i, n, 2 * (i % 2), hT)
                if i % 2:
                    free_slot(n)
                if i % 2 and i > 1:
                    ada2_columns(i // 2 - 1)
            pe.wait_ge(early_in, 16 * 6)
            for t in range(T):
                for k in range(KC):
                    mm = nc.tensor.matmul(bank[4][:, t * 16:(t + 1) * 16], hT[:, k, t * P:(t + 1) * P], wba[:, k, :],
                                          start=(k == 0), stop=(k == KC - 1))
            mm.then_inc(pe_ba, 1)
            arrived(chunk_no["pool"][0])
            for i in range(2):
                pair_of(12 + i, chunk_no["pool"][0], 2 * i, hT)
            free_slot(chunk_no["pool"][0])
            ada2_columns(5)
            for i in range(4):
                n = chunk_no["gate0"][i // 2]
                arrived(n)
                pair_of(14 + i, n, 2 * (i % 2), hT)
                if i % 2:
                    free_slot(n)
                    ada2_columns(6 + i // 2)
            pe.wait_ge(vec_g, 1)
            nc.tensor.matmul(bank[6][:, 0:16], const_tile("causal"), heads_in[:, G].rearrange("p t h -> p (t h)"),
                             start=True, stop=True).then_inc(pe_g, 1)
            pe.wait_ge(vec_pooled, 1)
            pe.wait_ge(act_ba, 1)
            for i in range(2):
                for a in range(2):
                    mm = nc.tensor.matmul(pair(4 + i)[:, a, :], pw[:, 2 * i + a, :], pool_b[:, 2 * i + a, :],
                                          start=True, stop=True)
            mm.then_inc(pe_ypool, 1)
            pe.wait_ge(vec_g, 2)
            nc.tensor.matmul(bank[6][:, 0:16], const_tile("after"), heads_in[:, G].rearrange("p t h -> p (t h)"),
                             start=True, stop=True).then_inc(pe_g, 1)
            pe.wait_ge(vec_ypool, 1)
            pick = const_tile("pick")
            for i in range(8):
                pe.wait_ge(pool_sq, i + 1)
                for a in range(2):
                    head = 2 * i + a
                    mm = nc.tensor.matmul(bank[4][0:2 * HEADS, 0:S],
                                          pick[:, 2 * HEADS - 1 - head:4 * HEADS - 1 - head],
                                          sq[:, i, a * S:(a + 1) * S], start=(head == 0), stop=(head == 2 * HEADS - 1))
            mm.then_inc(pe_ssq, 1)
            n = chunk_no["pool_out"][0]
            arrived(n)
            wp = slot_as(n % RING, 4)

            def pool_out_pair(i):
                pair_of(18 + i, n, 0, y_pool, 4, lambda k, a: wp[:, k, (2 * i + a) * P:(2 * i + a + 1) * P])

            pool_out_pair(0)
            pe.wait_ge(vec_rnorm, 1)
            for i in range(8):
                if i >= 2:
                    pe.wait_ge(vec_norm, i - 1)
                for a in range(2):
                    head = 2 * i + a
                    mm = nc.tensor.matmul(pair(4 + i % 2)[:, a, :],
                                          ident[0:2 * HEADS, head:head + 1].to_broadcast([2 * HEADS, P]), norms,
                                          start=True, stop=True)
                mm.then_inc(pe_norm, 1)
            for i in range(1, 4):
                pool_out_pair(i)
            free_slot(n)

            def z_pair(i):
                n = chunk_no["z"][i // 2]
                arrived(n)
                pe.wait_ge(*((act_z, i) if i else (vec_mod2, 1)))
                for a in range(2):
                    mm = project(pair(7)[:, a, :], n, 2 * (i % 2) + a, hT)
                mm.then_inc(pe_z, 1)
                if i % 2:
                    free_slot(n)

            def gate1_pair(i):
                n = chunk_no["gate1"][i // 2]
                arrived(n)
                if i == 1:
                    pe.wait_ge(act_z, 4)
                if i > 1:
                    pe.wait_ge(act_gate1, i - 1)
                for a in range(2):
                    mm = project(pair(6 + i % 2)[:, a, :], n, 2 * (i % 2) + a, hT)
                mm.then_inc(pe_gate1, 1)
                if i % 2:
                    free_slot(n)

            pe.wait_ge(vec_pair, 6)
            for g in range(2):
                hs = [HG * g + h for h in range(HG)]
                for t in range(T):
                    b = 2 * g + t
                    tok = slice(t * P, (t + 1) * P)
                    if g:
                        pe.wait_ge(vec_o, 2 * g - 1 + t)
                        pe.wait_ge(vec_state, 3 * g)
                    pe.wait_ge(vec_norm, 8)
                    for h in hs:
                        nc.tensor.matmul(quad(3 * t + 1)[:, h % HG], k_of[:, h, tok], k_of[:, h, tok],
                                         start=True, stop=True)
                    for h in hs:
                        mm = nc.tensor.matmul(quad(3 * t + 2)[:, h % HG], k_of[:, h, tok], q_of[:, h, tok],
                                              start=True, stop=True)
                    mm.then_inc(pe_kk, 1)
                    pe.wait_ge(vec_diag, b + 1)
                    nc.tensor.matmul(bank[3 * t][:, :], ones, prod[:, t].rearrange("p h n -> p (h n)"),
                                     start=True, stop=True).then_inc(pe_grow, 1)
                z_pair(2 * g)
                z_pair(2 * g + 1)
                for t in range(T):
                    b = 2 * g + t
                    tok = slice(t * P, (t + 1) * P)
                    pe.wait_ge(vec_l, b + 1)
                    for h in hs:
                        mm = nc.tensor.transpose(quad(3 * t)[:, h % HG], decay[:, t, h % HG], ident)
                    mm.then_inc(pe_lT, 1)
                    for h in hs:
                        nc.tensor.transpose(quad(3 * t + 1)[:, h % HG], k_of[:, h, tok], ident)
                    for h in hs:
                        mm = nc.tensor.transpose(quad(3 * t + 2)[:, h % HG], v_of[:, h, tok], ident)
                    mm.then_inc(pe_nat, 1)
                for i in range(5):
                    for t in range(T):
                        pe.wait_ge(pool_off, 14 * g + 4 + 2 * i + t + 1)
                        pe.wait_ge(vec_inv, 12 * g + 2 * i + t + 1)
                        if i == 0:
                            pe.wait_ge(vec_nat, 2 * g + t + 1)
                        for h in range(HG):
                            mm = nc.tensor.matmul(quad(3 * t + 1)[:, h], off[:, t, h], inv[:, t, h],
                                                  start=True, stop=True)
                        mm.then_inc(pe_prod, 1)
                    for t in range(T):
                        pe.wait_ge(act_prod, 10 * g + 2 * i + t + 1)
                        if i < 4:
                            for h in range(HG):
                                nc.tensor.matmul(quad(3 * t)[:, h], invT[:, t, h], prod[:, t, h],
                                                 start=True, stop=True)
                        for h in range(HG):
                            mm = nc.tensor.matmul(quad(3 * t + 2)[:, h], prod[:, t, h], invT[:, t, h],
                                                  start=True, stop=True)
                        mm.then_inc(pe_corr, 1)
                for t in range(T):
                    pe.wait_ge(vec_inv, 12 * g + 10 + t + 1)
                    for h in range(HG):
                        nc.tensor.matmul(quad(3 * t)[:, h], invT[:, t, h], vb[:, t, h], start=True, stop=True)
                    for h in range(HG):
                        mm = nc.tensor.matmul(quad(3 * t + 1)[:, h], kbg[:, t, h], invT[:, t, h],
                                              start=True, stop=True)
                    mm.then_inc(pe_uw, 1)
                for ci in range(S // CHUNK):
                    t, lo = ci // 2, CHUNK * (ci % 2)
                    rows_c = slice(lo, lo + CHUNK)
                    tok = slice(t * P + lo, t * P + lo + CHUNK)
                    if ci % 2 == 0:
                        pe.wait_ge(act_u, 2 * g + t + 1)
                        pe.wait_ge(vec_w, 2 * g + t + 1)
                    if ci:
                        pe.wait_ge(vec_state, 3 * g + ci)
                        for h in range(HG):
                            mm = nc.tensor.matmul(quad(3 * t)[rows_c, h], kbg[:, t, h, rows_c], state[:, h],
                                                  start=True, stop=True)
                        mm.then_inc(pe_ws, 1)
                    if g:
                        gate1_pair(ci)
                    if ci:
                        pe.wait_ge(vec_vnew, 3 * g + ci)
                    for h in range(HG):
                        if ci:
                            nc.tensor.matmul(quad(3 * t + 1)[rows_c, h], q_of[:, HG * g + h, tok], state[:, h],
                                             start=True, stop=False)
                        mm = nc.tensor.matmul(quad(3 * t + 1)[rows_c, h], decayT[rows_c, t, h, rows_c],
                                              vb[rows_c, t, h], start=(ci == 0), stop=True)
                    if ci < S // CHUNK - 1:
                        for h in range(HG):
                            mm = nc.tensor.matmul(quad(3 * t + 2)[:, h], kdec[rows_c, t, h], vb[rows_c, t, h],
                                                  start=True, stop=True)
                    mm.then_inc(pe_o, 1)

            def tail_pair(i, n, b, rhs):
                for a in range(2):
                    mm = project(pair(b)[:, a, :], n, 2 * (i % 2) + a, rhs)
                mm.then_inc(pe_tail, 1)
                if i % 2:
                    free_slot(n)

            pe.wait_ge(vec_o, 4)
            pe.wait_ge(vec_state, 6)
            pe.wait_ge(vec_on, 4)
            for h in range(HEADS):
                for t in range(T):
                    mm = nc.tensor.transpose(pair(h // 2)[:, h % 2, t * P:(t + 1) * P],
                                             o_nat[:, h // HG, t, h % HG], ident)
            mm.then_inc(pe_oT, 1)
            pe.wait_ge(vec_yg, 4)
            for i in range(4):
                n = chunk_no["gdn_out"][i // 2]
                arrived(n)
                tail_pair(i, n, i, region_z)
            pe.wait_ge(act_gate1, 4)
            pe.wait_ge(vec_tail, 4)
            for i in range(4):
                n = chunk_no["w_out"][i // 2]
                arrived(n)
                tail_pair(i, n, 4 + i, region_y)
            pe.wait_ge(vec_tail, 8)
            for t in range(T):
                for half in range(2):
                    for j in range(4):
                        f = 4 * half + j
                        mm = nc.tensor.transpose(bank[2 * t + half][:, j * P:(j + 1) * P],
                                                 moT[:, f, t * P:(t + 1) * P], ident)
                        if j == 0:
                            carry(mm)
                    mm.then_inc(pe_mo, 1)
            pe.wait_ge(vec_xn2, 2)
            for f in range(KC):
                for t in range(T):
                    mm = nc.tensor.transpose(pair(4 + f // 2)[:, f % 2, t * P:(t + 1) * P],
                                             xn2[:, t, f * P:(f + 1) * P], ident)
                if f % 2:
                    mm.then_inc(pe_h2T, 1)
            pe.wait_ge(vec_h2T, 1)
            for t in range(T):
                for half in range(2):
                    for j in range(4):
                        f = 4 * half + j
                        mm = nc.tensor.transpose(bank[2 * t + half][:, j * P:(j + 1) * P],
                                                 h2T[:, f, t * P:(t + 1) * P], ident)
                    mm.then_inc(pe_h2, 1)
            for t in range(T):
                for k in range(KC):
                    mm = nc.tensor.matmul(bank[4][:, t * E:(t + 1) * E], h2T[:, k, t * P:(t + 1) * P], rw[:, k, :],
                                          start=(k == 0), stop=(k == KC - 1))
            mm.then_inc(pe_logits, 1)
            pe.wait_ge(vec_mask, 1)
            for t in range(T):
                nc.tensor.matmul(bank[5][:, t * E:(t + 1) * E], const_tile("before"), mask[:, t, :],
                                 start=True, stop=(t == 0))
                if t:
                    nc.tensor.matmul(bank[5][:, t * E:(t + 1) * E], ones, mask[:, 0, :], start=False, stop=True)
            for t in range(T):
                mm = nc.tensor.matmul(bank[6][0:E, 0:1], mask[:, t, :], ones[:, 0:1], start=(t == 0), stop=(t == 1))
            mm.then_inc(pe_rank, 1)
            pe.wait_ge(vec_diag2, 1)
            pe.wait_ge(act_h2, 4)
            for half in range(2):
                mm = nc.tensor.matmul(bank[half][:, :], ones,
                                      gt2_diag[:, 4 * half:4 * half + 4, :].rearrange("p f n -> p (f n)"),
                                      start=True, stop=True)
            mm.then_inc(pe_gt2, 1)
            pe.wait_ge(vec_counts, 1)
            nc.tensor.matmul(bank[6][:, 32:32 + E], blocks_row, const_tile("causal")[0:E, 0:E],
                             start=True, stop=True).then_inc(pe_ends, 1)
            pe.wait_ge(vec_gatew, 1)
            for t in range(T):
                mm = nc.tensor.transpose(bank[2][0:E, t * P:(t + 1) * P], gatew[:, t, :], ident)
            mm.then_inc(pe_gatewT, 1)
            pe.wait_ge(vec_blocks, 1)
            for i in range(2):
                mm = nc.tensor.transpose(bank[6][0:1, 64 + i * P:64 + (i + 1) * P], block_cols[:, i:i + 1], ident)
            mm.then_inc(pe_blocks, 1)
            pe.wait_ge(vec_route, 1)
            for t in range(T):
                for half in range(2):
                    nc.tensor.matmul(bank[4 + 2 * t + half][:, :], ident, xt[:, t, half * 512:(half + 1) * 512],
                                     start=True, stop=False, skip_group_check=True)

            pe.wait_ge(vec_b2, 1)
            for t in range(T):
                for half in range(2):
                    nc.tensor.matmul(bank[4 + 2 * t + half][:, :], gatewT[:, t * P:(t + 1) * P],
                                     b2_rows[:, half * 512:(half + 1) * 512],
                                     start=False, stop=False, skip_group_check=True)

            def stream_chunk(out_bank, tokens, slot, first_k):
                for k in range(KC):
                    for h in range(2):
                        mm = nc.tensor.matmul(out_bank[h * SLOTS:(h + 1) * SLOTS, 0:HALF], tokens[:, k, :],
                                              ring[:, slot, k, h * HALF:(h + 1) * HALF],
                                              start=(first_k and k == 0), stop=(k == KC - 1))
                mm.then_inc(used[slot], 1)

            def w1_chunk(n, j):
                pe.wait_ge(landed[j], 16 * (n + USES + 1))
                if j < 2:
                    at_least(pe, vec_y, 2 * n - 1 + j)
                else:
                    pe.wait_ge(vec_hu, 8 * n + 2 * j - 2)
                for h in range(2):
                    lo = j * CW + h * HALF
                    nc.tensor.matmul(bank[j % 2][h * SLOTS:(h + 1) * SLOTS, 0:HALF], onehot,
                                     b1_rows[:, lo:lo + HALF], start=True, stop=False)
                stream_chunk(bank[j % 2], xT, j, False)

            def turn_hidden(n, j):
                pe.wait_ge(vec_act, 4 * n + j + 1)
                if j < 3:
                    at_least(pe, act_actT, 4 * n + j)
                else:
                    pe.wait_ge(act_selT, n + 1)
                nc.tensor.transpose(bank[3][:, 256:384], act_nat[:, j % 2, :], ident).then_inc(pe_actT, 1)

            def gather(count):
                pe.wait_ge(vec_sel, count)
                at_least(pe, act_xT, count - 1)
                for f in range(KC):
                    for t in range(T):
                        mm = nc.tensor.matmul(bank[2][:, f * SLOTS:(f + 1) * SLOTS],
                                              h2[:, t, f * P:(f + 1) * P], sel[:, t, :],
                                              start=(t == 0), stop=(t == T - 1))
                mm.then_inc(pe_gather, 1)

            def serve(n):
                pe.wait_ge(act_xT, n + 1)
                pe.wait_ge(vec_onehot, n + 1)
                w1_chunk(n, 0)
                w1_chunk(n, 1)
                turn_hidden(n, 0)
                w1_chunk(n, 2)
                turn_hidden(n, 1)
                w1_chunk(n, 3)
                turn_hidden(n, 2)
                gather(n + 2)
                pe.wait_ge(vec_wsel, n + 1)
                pe.wait_ge(act_actT, 4 * n + 3)
                for t in range(T):
                    mm = nc.tensor.matmul(bank[3][0:SLOTS, t * P:(t + 1) * P], wsel[:, t, :], ident,
                                          start=True, stop=True)
                mm.then_inc(pe_selT, 1)
                turn_hidden(n, 3)
                for j in range(2):
                    pe.wait_ge(landed[4 + j], 16 * (n + USES + 1))
                    pe.wait_ge(vec_hu, 8 * n + 6 + 2 * j)
                    if j == 0:
                        pe.wait_ge(act_actT, 4 * n + 4)
                    stream_chunk(bank[j], actT, 4 + j, True)
                for half in range(2):
                    pe.wait_ge(vec_y, 2 * n + half + 1)
                    for t in range(T):
                        nc.tensor.matmul(bank[4 + 2 * t + half][:, :], wselT[:, t * P:(t + 1) * P],
                                         y_nat[:, half * 512:(half + 1) * 512],
                                         start=False, stop=False, skip_group_check=True)

            gather(1)
            serve(0)
            further_blocks(pe, serve)
            for i in range(4):
                mm = nc.tensor.matmul(bank[4 + i][:, 0:1], const_tile("before")[:, 0:P], const_tile("strict")[:, 127:128],
                                      start=False, stop=True, skip_group_check=True)
            mm.then_inc(pe_moe, 1)

        @block.vector
        def _(dve):
            chain = [0]

            def link(*steps):
                for ins in steps:
                    chain[0] += 1
                    ins.then_inc(vec_chain, 1)
                dve.wait_ge(vec_chain, chain[0])

            tt, ts, stt = nc.vector.tensor_tensor, nc.vector.tensor_scalar, nc.vector.scalar_tensor_tensor
            copy, recip = nc.vector.tensor_copy, nc.vector.reciprocal

            link(nc.vector.memset(small[:, 16:17], EPS))
            dve.wait_ge(const_in, 16)
            ts(small[:, 17:18], const_tile("qscale"), EPS, None, ALU.mult)
            dve.wait_ge(pe_rows, 1)
            copy(cols[:, :], bank[6][:, 0:ROWS]).then_inc(vec_cols, 1)
            copy(conv_cols[:, :, :], bank[6][:, 128:128 + 96].rearrange("p (j b) -> p j b", j=TAPS)).then_inc(vec_cols, 1)
            dve.wait_ge(vec_cols, 2)
            dve.wait_ge(act_xrms, 1)
            link(recip(stat[:, 0, 2:4], stat[:, 0, 2:4]))
            for t in range(T):
                ts(xt[:, t, :], xt[:, t, :], stat[:, 0, 2 + t:3 + t], None, ALU.mult).then_inc(vec_xn, 1)
            def ada_sums(n, place):
                dve.wait_ge(landed[place % RING], 16 * (place // RING + 1))
                if n > 1:
                    dve.wait_ge(pe_ada, n - 1)
                w = ring[:, place % RING, :, :]
                for k in range(KC):
                    half = ada_sum[:, n % 2, k % 2, :]
                    if k > 1:
                        dve.wait_ge(vec_adastep, KC * n + k - 1)
                        ins = stt(half, w[:, k, :], c_act[:, k:k + 1], half, ALU.mult, ALU.add)
                    else:
                        ins = ts(half, w[:, k, :], c_act[:, k:k + 1], None, ALU.mult)
                    ins.then_inc(vec_adastep, 1)
                dve.wait_ge(vec_adastep, KC * n + KC)
                tt(ada_sum[:, n % 2, 0, :], ada_sum[:, n % 2, 0, :], ada_sum[:, n % 2, 1, :], ALU.add)\
                    .then_inc(vec_ada, 1)

            dve.wait_ge(act_c, 1)
            for n in range(4):
                ada_sums(n, chunk_no["ada"][n])
            dve.wait_ge(pe_ada, 4)
            link(tt(mod[:, 0:16], bank[5][:, 0:16], cols[:, 0:16], ALU.add))
            link(stt(scale1[:, :], mod[:, 8:16], 1.0, cols[:, ROW_G1:ROW_G1 + 8], ALU.add, ALU.mult))
            dve.wait_ge(pe_xT, 1)
            for f in range(KC):
                ins = ts(hT[:, f, :], pair(f // 2)[:, f % 2, :], scale1[:, f:f + 1], mod[:, f:f + 1], ALU.mult, ALU.add)
            ins.then_inc(vec_hT, 1)

            for i in range(12):
                dve.wait_ge(pe_pair, i + 1)
                src = pair(i % 4)
                for j in range(TAPS - 1, -1, -1):
                    shift = TAPS - 1 - j
                    steps = []
                    for a in range(2):
                        f = 2 * i + a
                        w = conv_cols[:, j, f:f + 1]
                        if shift == 0:
                            steps.append(ts(qkv[:, f, :], src[:, a, :], w, None, ALU.mult))
                        else:
                            steps.append(stt(qkv[:, f, shift:S], src[:, a, 0:S - shift], w, qkv[:, f, shift:S],
                                             ALU.mult, ALU.add))
                    if j:
                        link(*steps)
                    else:
                        steps[1].then_inc(vec_conv, 1)
                if i % 2:
                    ada_sums(4 + i // 2, chunk_no["ada2"][i // 2])
            for m in (6, 7):
                ada_sums(4 + m, chunk_no["ada2"][m])
            dve.wait_ge(pe_ba, 1)
            dve.wait_ge(early_in, 16 * 6)
            tt(heads_in[:, APLUS], bank[4][:, 0:32].rearrange("p (t n) -> p t n", t=T)[:, :, 8:16],
               small[:, 0:8].unsqueeze(1).to_broadcast([P, T, HEADS]), ALU.add).then_inc(vec_ba, 1)
            dve.wait_ge(vec_ba, 1)
            stt(heads_in[:, MAG], heads_in[:, APLUS], -1.0, heads_in[:, APLUS], ALU.mult, ALU.max).then_inc(vec_ba, 1)
            for i in range(2):
                dve.wait_ge(pe_pair, 12 + i + 1)
                copy(u_pool[:, 2 * i:2 * i + 2, :], pair(i)).then_inc(vec_pair, 1)
            dve.wait_ge(vec_pair, 2)
            src, held = u_pool, (pool_a, pool_b)
            for i in range(4):
                dst, w = held[i % 2], 2 ** i
                link(tt(dst[:, i:4, w:S], src[:, i:4, w:S], src[:, i:4, 0:S - w], ALU.add),
                     copy(dst[:, i:4, 0:w], src[:, i:4, 0:w]))
                src = dst
            counts = const_tile("count").rearrange("p (g n) -> p g n", g=4)
            dve.wait_ge(const_in, 16)
            for i, w in enumerate(WINDOWS):
                src = held[i % 2]
                link(tt(pool_b[:, i, 0:16], src[:, i, 0:16], counts[:, i, :], ALU.mult),
                     stt(pool_b[:, i, 16:S], src[:, i, 16:S], 1.0 / w, u_pool[:, i, 16:S], ALU.mult, ALU.subtract))
            tt(pool_b[:, :, 0:16], pool_b[:, :, 0:16], u_pool[:, :, 0:16], ALU.subtract).then_inc(vec_pooled, 1)

            dve.wait_ge(act_ba, 2)
            u, denom, z, z2, acc = (heads_in[:, what] for what in (EMAG, ONEP, LN1P, MAG, KDF))
            link(ts(denom, u, 2.0, None, ALU.add))
            link(recip(denom, denom), ts(heads_in[:, APLUS], heads_in[:, APLUS], 0.0, None, ALU.max))
            link(tt(z, u, denom, ALU.mult))
            link(tt(z2, z, z, ALU.mult))
            link(ts(acc, z2, 1.0 / 17, None, ALU.mult))
            for odd in range(15, 1, -2):
                link(stt(acc, acc, 1.0 / odd, z2, ALU.add, ALU.mult))
            link(stt(acc, acc, 1.0, z, ALU.add, ALU.mult))
            link(stt(heads_in[:, LN1P], acc, 2.0, heads_in[:, APLUS], ALU.mult, ALU.add))
            stt(heads_in[:, G], heads_in[:, LN1P], -1.0, small[:, 24:32].unsqueeze(1).to_broadcast([P, T, HEADS]),
                ALU.mult, ALU.mult).then_inc(vec_g, 1)
            dve.wait_ge(pe_g, 1)
            rates = bank[6][:, 0:16].rearrange("p (t h) -> p t h", t=T)
            copy(heads_in[:, GC], rates).then_inc(vec_g, 1)
            dve.wait_ge(pe_ypool, 1)
            for i in range(4):
                ins = ts(y_pool[:, i, :], pair(4 + i // 2)[:, i % 2, :], cols[:, ROW_POOL + i:ROW_POOL + i + 1], None,
                         ALU.mult)
            ins.then_inc(vec_ypool, 1)
            dve.wait_ge(pe_g, 2)
            dve.wait_ge(vec_g, 2)
            copy(heads_in[:, KDF], rates).then_inc(vec_g, 1)
            dve.wait_ge(pe_ada, 12)
            link(tt(mod[:, 16:48], bank[7][:, 0:32], cols[:, 16:48], ALU.add))
            stt(scale2[:, :], mod[:, 32:40], 1.0, cols[:, ROW_G2:ROW_G2 + 8], ALU.add, ALU.mult).then_inc(vec_mod2, 1)
            dve.wait_ge(act_norm, 1)
            recip(norms, norms).then_inc(vec_rnorm, 1)
            for i in range(8):
                dve.wait_ge(pe_norm, i + 1)
                a = qkv[:, 2 * i:2 * i + 2, :]
                tt(a, a, pair(4 + i % 2), ALU.mult).then_inc(vec_norm, 1)
            for i in range(4):
                dve.wait_ge(pe_pair, 18 + i + 1)
                a = region_y[:, 2 * i:2 * i + 2, :]
                dve.wait_ge(act_pair, i + 1)
                tt(a, a, pair((18 + i) % 4), ALU.mult).then_inc(vec_pair, 1)
            dve.wait_ge(act_ba, 3)
            link(tt(heads_in[:, BEG], heads_in[:, BETA], heads_in[:, EG], ALU.mult))

            def norm_output(b):
                dve.wait_ge(act_orms, b + 1)
                rms = small[:, 32 + HG * b:32 + HG * (b + 1)]
                link(recip(rms, rms))
                a = o_flat[:, b, :].rearrange("p (h n) -> p h n", h=HG)
                tt(a, a, per_head(rms), ALU.mult).then_inc(vec_on, 1)

            dve.wait_ge(vec_g, 3)
            dve.wait_ge(vec_norm, 8)
            for g in range(2):
                def head(what, t, h):
                    return heads_in[:, what, t, HG * g + h:HG * g + h + 1]

                def heads(what, t):
                    return per_head(heads_in[:, what, t, HG * g:HG * g + HG])

                for t in range(T):
                    for h in range(HG):
                        ins = ts(prod[:, t, h], ident, head(GC, t, h), None, ALU.mult)
                    ins.then_inc(vec_diag, 1)
                for t in range(T):
                    dve.wait_ge(pe_grow, 2 * g + t + 1)
                    for h in range(HG):
                        ts(decay[:, t, h], quad(3 * t)[:, h], head(GC, t, h), 0.0, ALU.subtract, ALU.max)
                    for h in range(HG):
                        ins = ts(decayT[:, t, h], quad(3 * t)[:, h], head(GC, t, h), 0.0, ALU.subtract, ALU.min)
                    ins.then_inc(vec_darg, 1)
                for t in range(T):
                    dve.wait_ge(pe_kk, 2 * g + t + 1)
                    dve.wait_ge(pool_decay, 2 * g + t + 1)
                    tt(decayT[:, t], quad(3 * t + 2), decayT[:, t], ALU.mult)
                    a = q_of[:, HG * g:HG * g + HG, t * P:(t + 1) * P]
                    tt(a, a, eg_row[:, t], ALU.mult)
                    for h in range(HG):
                        ins = stt(decay[:, t, h], quad(3 * t + 1)[:, h], head(BETA, t, h), decay[:, t, h],
                                  ALU.mult, ALU.mult)
                    ins.then_inc(vec_l, 1)
                for t in range(T):
                    dve.wait_ge(pe_lT, 2 * g + t + 1)
                    copy(lT[:, t], quad(3 * t)).then_inc(vec_lT, 1)
                for t in range(T):
                    dve.wait_ge(pe_nat, 2 * g + t + 1)
                    tt(vb[:, t], quad(3 * t + 2), heads(BETA, t), ALU.mult)
                    tt(kbg[:, t], quad(3 * t + 1), heads(BEG, t), ALU.mult)
                    tt(kdec[:, t], quad(3 * t + 1), heads(KDF, t), ALU.mult).then_inc(vec_nat, 1)
                for t in range(T):
                    dve.wait_ge(pool_off, 14 * g + 2 * t + 1)
                    stt(inv[:, t], inv[:, t], -1.0, over_heads(ident), ALU.mult, ALU.add)
                    dve.wait_ge(pool_off, 14 * g + 2 * t + 2)
                    stt(invT[:, t], invT[:, t], -1.0, over_heads(ident), ALU.mult, ALU.add).then_inc(vec_inv, 1)
                for i in range(5):
                    for t in range(T):
                        dve.wait_ge(vec_inv, 12 * g + 2 * i + t + 1)
                        dve.wait_ge(pe_corr, 10 * g + 2 * i + t + 1)
                        if i < 4:
                            tt(inv[:, t], inv[:, t], quad(3 * t), ALU.subtract)
                        tt(invT[:, t], invT[:, t], quad(3 * t + 2), ALU.subtract).then_inc(vec_inv, 1)
                for t in range(T):
                    dve.wait_ge(act_u, 2 * g + t + 1)
                    copy(kbg[:, t], quad(3 * t + 1)).then_inc(vec_w, 1)
                dve.wait_ge(act_u, 2 * g + 2)
                for ci in range(S // CHUNK):
                    t, lo = ci // 2, CHUNK * (ci % 2)
                    rows_c = slice(lo, lo + CHUNK)
                    if g:
                        for b in ((), (0, 1), (), (2,))[ci]:
                            norm_output(b)
                    if ci:
                        dve.wait_ge(pe_ws, 3 * g + ci)
                        tt(vb[rows_c, t], vb[rows_c, t], quad(3 * t)[rows_c], ALU.subtract).then_inc(vec_vnew, 1)
                        dve.wait_ge(vec_state, 3 * g + ci)
                    dve.wait_ge(pe_o, 4 * g + ci + 1)
                    if ci == 0:
                        copy(state, quad(3 * t + 2)).then_inc(vec_state, 1)
                    elif ci < S // CHUNK - 1:
                        for h in range(HG):
                            ins = stt(state[:, h], state[:, h], eg_row[:, t, h, lo + CHUNK - 1:lo + CHUNK],
                                      quad(3 * t + 2)[:, h], ALU.mult, ALU.add)
                        ins.then_inc(vec_state, 1)
                    if ci % 2:
                        copy(o_nat[:, g, t], quad(3 * t + 1)).then_inc(vec_o, 1)
                    if g:
                        for b in ((0, 1), (), (2,), (3,))[ci]:
                            dve.wait_ge(pool_osq, b + 1)
                            nc.vector.tensor_reduce(small[:, 32 + HG * b:32 + HG * (b + 1)],
                                                    o_sq[:, b, :].rearrange("p (h n) -> p h n", h=HG),
                                                    AX.X, ALU.add).then_inc(vec_ossq, 1)
            norm_output(3)
            dve.wait_ge(pe_oT, 1)
            dve.wait_ge(act_z, 4)
            for i in range(4):
                a = region_z[:, 2 * i:2 * i + 2, :]
                stt(a, pair(i), cols[:, ROW_GDN:ROW_GDN + 1], a, ALU.mult, ALU.mult).then_inc(vec_yg, 1)
            for i in range(4):
                dve.wait_ge(pe_tail, i + 1)
                dve.wait_ge(act_gate1, i + 1)
                a, y = gate1[:, 2 * i:2 * i + 2, :], region_y[:, 2 * i:2 * i + 2, :]
                link(tt(a, a, pair(i), ALU.mult))
                tt(y, y, a, ALU.add).then_inc(vec_tail, 1)
            for i in range(4):
                dve.wait_ge(pe_tail, 4 + i + 1)
                for f in (2 * i, 2 * i + 1):
                    ins = ts(moT[:, f, :], pair(4 + i)[:, f % 2, :], mod[:, 16 + f:17 + f], None, ALU.mult)
                ins.then_inc(vec_tail, 1)
            dve.wait_ge(x_in, 16 * 2 * T)
            for t in range(T):
                for half in range(2):
                    dve.wait_ge(pe_mo, 2 * t + half + 1)
                    a = xt[:, t, half * 512:(half + 1) * 512]
                    tt(a, a, bank[2 * t + half][:, :], ALU.add).then_inc(vec_x1, 1)
            dve.wait_ge(vec_x1, 4)
            dve.wait_ge(act_x1sq, 3)
            link(recip(stat[:, 1, 2:4], stat[:, 1, 2:4]))
            for t in range(T):
                ts(xn2[:, t, :], xt[:, t, :], stat[:, 1, 2 + t:3 + t], None, ALU.mult).then_inc(vec_xn2, 1)
            dve.wait_ge(vec_mod2, 1)
            for f in range(KC):
                dve.wait_ge(pe_h2T, f // 2 + 1)
                ins = ts(h2T[:, f, :], pair(4 + f // 2)[:, f % 2, :], scale2[:, f:f + 1], mod[:, 24 + f:25 + f],
                         ALU.mult, ALU.add)
            ins.then_inc(vec_h2T, 1)

            for f in range(KC):
                ins = ts(gt2_diag[:, f, :], ident, mod[:, 40 + f:41 + f], None, ALU.mult)
            ins.then_inc(vec_diag2, 1)

            dve.wait_ge(pe_logits, 1)
            link(tt(logits, bank[4][:, 0:2 * E].rearrange("p (t e) -> p t e", t=T),
                    rb[:, :].unsqueeze(1).to_broadcast([P, T, E]), ALU.add))
            link(*(nc.vector.max(top[:, t, :], logits[:, t, :]) for t in range(T)))
            link(*(nc.vector.max_index(top_i[:, t, :], top[:, t, :], logits[:, t, :]) for t in range(T)))
            link(copy(idx, top_i[:, :, :]))
            for t in range(T):
                ins = ts(expw[:, t, 0:4], top[:, t, 0:4], top[:, t, 0:1], None, ALU.subtract)
            ins.then_inc(vec_logits, 1)
            lanes = const_tile("iota")[:, 0:E]
            link(*(ts(mask[:, t, :], lanes, idx[:, t, 0:1], None, ALU.is_equal) for t in range(T)))
            for rk in range(1, TOPK):
                steps = [stt(mask[:, t, :], lanes, idx[:, t, rk:rk + 1], mask[:, t, :], ALU.is_equal, ALU.add)
                         for t in range(T)]
                if rk < TOPK - 1:
                    link(*steps)
                else:
                    steps[-1].then_inc(vec_mask, 1)
            dve.wait_ge(act_top, 1)
            link(nc.vector.tensor_reduce(expw[:, :, 4:5], expw[:, :, 0:4], AX.X, ALU.add))
            link(recip(expw[:, :, 4:5], expw[:, :, 4:5]))
            link(tt(expw[:, :, 0:4], expw[:, :, 0:4], expw[:, :, 4:5].to_broadcast([P, T, 4]), ALU.mult))
            link(*(ts(gatew[:, t, :], lanes, idx[:, t, 0:1], expw[:, t, 0:1], ALU.is_equal, ALU.mult) for t in range(T)))
            for rk in range(1, TOPK):
                link(*(ts(hot[:, t, :], lanes, idx[:, t, rk:rk + 1], expw[:, t, rk:rk + 1], ALU.is_equal, ALU.mult)
                       for t in range(T)))
                if rk < TOPK - 1:
                    link(tt(gatew, gatew, hot, ALU.add))
                else:
                    tt(gatew, gatew, hot, ALU.add).then_inc(vec_gatew, 1)
            dve.wait_ge(pe_rank, 1)
            dve.wait_ge(vec_mask, 1)
            link(stt(slot_of, bank[5][:, 0:2 * E].rearrange("p (t e) -> p t e", t=T), 1.0, mask, ALU.add, ALU.mult),
                 ts(counts_e[:, 0:1], bank[6][0:E, 0:1], float(SLOTS), 1.0, ALU.is_gt, ALU.add))
            for k in range(2, -(-S // SLOTS)):
                link(ts(counts_e[:, 1:2], bank[6][0:E, 0:1], float(SLOTS * k), None, ALU.is_gt))
                link(tt(counts_e[:, 0:1], counts_e[:, 0:1], counts_e[:, 1:2], ALU.add))
            ts(blocks_row, ones[0:E, :], counts_e[:, 0:1], None, ALU.mult).then_inc(vec_counts, 1)
            link(ts(slot_of, slot_of, -1.0, None, ALU.add))
            dve.wait_ge(pe_ends, 1)
            row = const_tile("row")
            link(ts(upto, bank[6][:, 32:32 + E], row, None, ALU.is_le))
            link(tt(ends, bank[6][:, 32:32 + E], upto, ALU.mult))
            link(nc.vector.tensor_reduce(block_cols[:, 0:1], upto, AX.X, ALU.add),
                 nc.vector.tensor_reduce(block_cols[:, 2:3], ends, AX.X, ALU.max))
            link(ts(block_cols[:, 0:1], block_cols[:, 0:1], float(E - 1), None, ALU.min),
                 tt(block_cols[:, 1:2], row, block_cols[:, 2:3], ALU.subtract))
            ts(block_cols[:, 1:2], block_cols[:, 1:2], float(SLOTS), float(S - SLOTS), ALU.mult, ALU.min)\
                .then_inc(vec_blocks, 1)
            dve.wait_ge(pe_gt2, 1)
            link(*(copy(gt2_row[:, half * 512:(half + 1) * 512], bank[half][:, :]) for half in range(2)))
            dve.wait_ge(b_in, 32)
            tt(b2_rows, b2_rows, gt2_row[0:E, :], ALU.mult)
            dve.wait_ge(pe_gatewT, 1)
            copy(gatewT, bank[2][0:E, 0:S]).then_inc(vec_b2, 1)
            dve.wait_ge(vec_b2, 1)
            dve.wait_ge(pe_blocks, 1)
            copy(blocks_i[:, 2 * P:2 * P + 1], bank[6][0:1, 32 + E - 1:32 + E])
            copy(blocks_i[:, 0:2 * P], bank[6][0:1, 64:64 + 2 * P]).then_inc(vec_route, 1)

            def select(e, start):
                for t in range(T):
                    ins = ts(sel[:, t, :], const_tile("iota")[:, bass.ds(start, SLOTS)],
                             slot_of[:, t, bass.ds(e, 1)], None, ALU.is_equal)
                ins.then_inc(vec_sel, 1)

            def mark(e):
                ts(onehot, ones[:, 0:SLOTS], ident[:, bass.ds(e, 1)], None, ALU.mult).then_inc(vec_onehot, 1)

            def serve(n):
                e, start = (0, 0) if isinstance(n, int) else (expert_of(dve, n), start_of(dve, n))
                e_next, start_next = expert_of(dve, n + 1), start_of(dve, n + 1)
                at_least(dve, pe_selT, n)
                for t in range(T):
                    ins = ts(wsel[:, t, :], const_tile("iota")[:, bass.ds(start, SLOTS)],
                             slot_of[:, t, bass.ds(e, 1)], gatew[:, t, bass.ds(e, 1)], ALU.is_equal, ALU.mult)
                ins.then_inc(vec_wsel, 1)
                dve.wait_ge(pe_gather, n + 1)
                select(e_next, start_next)
                for j in range(4):
                    m = 4 * n + j
                    dve.wait_ge(used[j], n + USES + 1)
                    at_least(dve, vec_act, m)
                    src = bank[j % 2][:, 0:HALF].rearrange("p (i a) -> p a i", a=2)
                    ts(hu[:, 0, :], src[:, 0, :], LIMIT, None, ALU.min).then_inc(vec_hu, 1)
                    ts(hu[:, 1, :], src[:, 1, :], LIMIT, -LIMIT, ALU.min, ALU.max).then_inc(vec_hu, 1)
                    dve.wait_ge(vec_hu, 2 * m + 2)
                    stt(hu[:, 1, :], hu[:, 1, :], 1.0, hu[:, 0, :], ALU.add, ALU.mult).then_inc(moe_chain, 1)
                    dve.wait_ge(moe_chain, m + 1)
                    dve.wait_ge(act_sig, m + 1)
                    at_least(dve, pe_actT, m - 1)
                    tt(act_nat[:, j % 2, :], hu[:, 1, :], sig, ALU.mult).then_inc(vec_act, 1)
                dve.wait_ge(pe_gather, n + 2)
                mark(e_next)
                for j in range(2):
                    dve.wait_ge(used[4 + j], n + USES + 1)
                    for h in range(2):
                        lo = j * CW + h * HALF
                        ins = tt(y_nat[:, lo:lo + HALF], bank[j][h * SLOTS:(h + 1) * SLOTS, 0:HALF],
                                 gt2_row[h * SLOTS:(h + 1) * SLOTS, lo:lo + HALF], ALU.mult)
                    ins.then_inc(vec_y, 1)

            select(0, 0)
            mark(0)
            dve.wait_ge(vec_route, 1)
            serve(0)
            further_blocks(dve, serve)
            dve.wait_ge(act_fin, 4)
            sums = stat[:, 0, :].rearrange("p (t a) -> p t a", t=T)
            tt(stat[:, 1, 0:2].unsqueeze(2), sums[:, :, 0:1], sums[:, :, 1:2], ALU.add).then_inc(vec_fin, 1)
            dve.wait_ge(act_fin, 5)
            recip(stat[:, 1, 2:4], stat[:, 1, 0:2]).then_inc(vec_fin, 1)
            dve.wait_ge(vec_fin, 2)
            dve.wait_ge(fin_in, 16)
            for t in range(T):
                for half in range(2):
                    cut_ = slice(half * 512, (half + 1) * 512)
                    ins = stt(fin[:, t, cut_], bank[4 + 2 * t + half][:, :], stat[:, 1, 2 + t:3 + t], fin_g[:, cut_],
                              ALU.mult, ALU.mult)
                ins.then_inc(vec_out, 1)


_INS = ["x", "c", "ada_w", "ada_b", "norm_mix_g", "norm_ffn_g", "w_in", "conv_w", "pool_w", "pool_scale", "a_log",
        "dt_bias", "gdn_norm_g", "w_pool_out", "w_gdn_out", "w_out", "router_w", "router_b", "exp_w1", "exp_b1",
        "exp_w2", "exp_b2", "final_norm_g"]
_OUT = (1, S, D)


def kernel(**inputs):
    import numpy as _np
    import concourse.bacc as _bacc
    from concourse import mybir as _mybir
    from concourse.bass_utils import run_bass_kernel_spmd as _run

    nc = _bacc.Bacc("TRN2", target_bir_lowering=False, num_devices=1)
    arrays, args = {}, []
    for name in _INS:
        a = _np.ascontiguousarray(inputs[name])
        arrays[f"in_{name}_dram"] = a
        args.append(nc.dram_tensor(f"in_{name}_dram", a.shape, _mybir.dt.from_np(a.dtype), kind="ExternalInput").ap())
    arrays["in_const_dram"] = constants()
    args.append(nc.dram_tensor("in_const_dram", (P, CONST_W), _mybir.dt.float32, kind="ExternalInput").ap())
    args.append(nc.dram_tensor("out_0_dram", _OUT, _mybir.dt.float32, kind="ExternalOutput").ap())
    program(nc, *args)
    r = _run(nc, [arrays], core_ids=[0])
    return r.results[0]["out_0_dram"]
```
